# Optimizing a Trainium2 kernel written in Bass

```python
import math
import jax
import jax.numpy as jnp
from jax import lax
import numpy as np
import jax, jax.numpy as jnp

D_MODEL = 1024
BATCH = 1
SEQ = 256
DEPTH = 2

NORM_EPS = 1e-6
D_FF = 2816
FFN_RES_SCALE = 0.5

A_HEADS = 8
A_HEAD_DIM = 64
A_PATTERNS = ((128, 1), (512, 4), (2048, 16))
A_BLOCK = 128

B_HEADS = 4
B_HEAD_DIM = 128
B_CONV = 4
B_CHUNK = 64

C_D_INNER = 2 * D_MODEL
C_HEAD_DIM = 64
C_HEADS = C_D_INNER // C_HEAD_DIM
C_GROUPS = 4
C_STATE = 128
C_CONV = 4
C_CHUNK = 64

A_WIDTH = A_HEADS * A_HEAD_DIM
B_WIDTH = B_HEADS * B_HEAD_DIM
EVEN_IN = 3 * A_WIDTH + 4 * B_WIDTH + 2 * B_HEADS
C_XBC = C_D_INNER + 2 * C_GROUPS * C_STATE
ODD_IN = C_D_INNER + C_XBC + C_HEADS
N_EVEN = (DEPTH + 1) // 2
N_ODD = DEPTH // 2


def rmsnorm(x, w):
    xf = x.astype(jnp.float32)
    y = xf * lax.rsqrt(jnp.mean(xf * xf, axis=-1, keepdims=True) + NORM_EPS)
    return (y * w.astype(jnp.float32)).astype(x.dtype)

def l2norm(x):
    return x * lax.rsqrt(jnp.sum(x * x, axis=-1, keepdims=True) + NORM_EPS)

def swiglu(x, w_gate, w_up, w_down):
    return (jax.nn.silu(x @ w_gate) * (x @ w_up)) @ w_down

def causal_dwconv(x, w):
    k_len, ch = w.shape
    return lax.conv_general_dilated(x, w[:, None, :].astype(x.dtype), window_strides=(1,),
                                    padding=((k_len - 1, 0),), dimension_numbers=('NWC', 'WIO', 'NWC'),
                                    feature_group_count=ch)

def dilated_window_attention(q, k, v):
    bsz, seq, heads, dh = q.shape
    scale = dh ** -0.5
    nums, maxes, dens = [], [], []
    for window, dil in A_PATTERNS:
        span = window // dil
        length = seq // dil
        blk = math.gcd(length, A_BLOCK)
        nb = length // blk

        def by_residue(t):
            return t.reshape(bsz, length, dil, heads, dh).transpose(0, 2, 1, 3, 4)

        pad = ((0, 0), (0, 0), (span, 0), (0, 0), (0, 0))
        kp = jnp.pad(by_residue(k), pad)
        vp = jnp.pad(by_residue(v), pad)
        idx = jnp.arange(nb)[:, None] * blk + jnp.arange(blk + span)[None, :]
        kb = kp[:, :, idx]
        vb = vp[:, :, idx]
        qb = by_residue(q).reshape(bsz, dil, nb, blk, heads, dh)
        s = jnp.einsum('brnqhd,brnkhd->brnhqk', qb, kb) * scale
        dist = jnp.arange(blk)[:, None] + span - jnp.arange(blk + span)[None, :]
        valid = ((dist >= 0) & (dist <= span))[None] & (idx >= span)[:, None, :]
        s = jnp.where(valid[:, None], s, -jnp.inf)
        m = jnp.max(s, axis=-1, keepdims=True)
        p = jnp.exp(s - m)
        den = jnp.sum(p, axis=-1)
        num = jnp.einsum('brnhqk,brnkhd->brnqhd', p, vb)

        def back(t):
            t = t.reshape(bsz, dil, length, *t.shape[4:])
            return jnp.moveaxis(t, 1, 2).reshape(bsz, seq, *t.shape[3:])

        nums.append(back(num))
        maxes.append(back(jnp.swapaxes(m[..., 0], -1, -2)))
        dens.append(back(jnp.swapaxes(den, -1, -2)))
    mx = jnp.max(jnp.stack(maxes), axis=0)
    wts = [jnp.exp(mi - mx) for mi in maxes]
    num = sum(n * w[..., None] for n, w in zip(nums, wts))
    den = sum(d * w for d, w in zip(dens, wts))
    return num / den[..., None]

def gated_delta_rule(q, k, v, g, beta):
    bsz, seq, heads, dk = q.shape
    dv = v.shape[-1]
    nc = seq // B_CHUNK

    def chunks(t):
        t = t.reshape(bsz, nc, B_CHUNK, heads, *t.shape[3:])
        return jnp.swapaxes(t, 2, 3)

    qc, kc, vc = chunks(q * dk ** -0.5), chunks(k), chunks(v)
    gc = jnp.cumsum(chunks(g), axis=-1)
    bc = chunks(beta)[..., None]
    tri = jnp.tril(jnp.ones((B_CHUNK, B_CHUNK), bool))
    strict = jnp.tril(jnp.ones((B_CHUNK, B_CHUNK), bool), -1)
    decay = jnp.exp(jnp.where(tri, gc[..., :, None] - gc[..., None, :], -jnp.inf))
    k_beta = kc * bc
    a_mat = jnp.where(strict, jnp.einsum('bnhid,bnhjd->bnhij', k_beta, kc) * decay, 0.0)
    t_mat = a_mat + jnp.eye(B_CHUNK, dtype=a_mat.dtype)
    u = lax.linalg.triangular_solve(t_mat, vc * bc, left_side=True, lower=True, unit_diagonal=True)
    w = lax.linalg.triangular_solve(t_mat, k_beta * jnp.exp(gc)[..., None], left_side=True, lower=True,
                                    unit_diagonal=True)
    qk = jnp.where(tri, jnp.einsum('bnhid,bnhjd->bnhij', qc, kc) * decay, 0.0)
    q_dec = qc * jnp.exp(gc)[..., None]
    g_last = gc[..., -1]
    k_dec = kc * jnp.exp(g_last[..., None] - gc)[..., None]

    def step(state, inp):
        u_i, w_i, q_i, qk_i, k_i, gl_i = inp
        v_new = u_i - jnp.einsum('bhck,bhkv->bhcv', w_i, state)
        o_i = jnp.einsum('bhck,bhkv->bhcv', q_i, state) + jnp.einsum('bhij,bhjv->bhiv', qk_i, v_new)
        state = state * jnp.exp(gl_i)[..., None, None] + jnp.einsum('bhck,bhcv->bhkv', k_i, v_new)
        return state, o_i

    xs = tuple(jnp.moveaxis(t, 1, 0) for t in (u, w, q_dec, qk, k_dec, g_last))
    state0 = jnp.zeros((bsz, heads, dk, dv), q.dtype)
    _, o = lax.scan(step, state0, xs)
    return jnp.transpose(o, (1, 0, 3, 2, 4)).reshape(bsz, seq, heads, dv)

def ssd_chunked_scan(x, a, b_in, c_in):
    bsz, seq, heads, p = x.shape
    groups, n = b_in.shape[2:]
    rep = heads // groups
    nc = seq // C_CHUNK
    xc = x.reshape(bsz, nc, C_CHUNK, groups, rep, p)
    acum = jnp.cumsum(a.reshape(bsz, nc, C_CHUNK, groups, rep), axis=2)
    bc = b_in.reshape(bsz, nc, C_CHUNK, groups, n)
    cc = c_in.reshape(bsz, nc, C_CHUNK, groups, n)
    tri = jnp.tril(jnp.ones((C_CHUNK, C_CHUNK), bool))[:, :, None, None]
    seg = jnp.exp(jnp.where(tri, acum[:, :, :, None] - acum[:, :, None, :], -jnp.inf))
    cb = jnp.einsum('bnlgd,bnsgd->bnlsg', cc, bc)
    y_diag = jnp.einsum('bnlsgr,bnsgrp->bnlgrp', cb[..., None] * seg, xc)

    def step(state, inp):
        x_i, a_i, b_i, c_i = inp
        y_off = jnp.einsum('blgd,bgrpd,blgr->blgrp', c_i, state, jnp.exp(a_i))
        a_last = a_i[:, -1]
        state = state * jnp.exp(a_last)[..., None, None] + jnp.einsum(
            'bsgd,bsgr,bsgrp->bgrpd', b_i, jnp.exp(a_last[:, None] - a_i), x_i)
        return state, y_off

    xs = tuple(jnp.moveaxis(t, 1, 0) for t in (xc, acum, bc, cc))
    state0 = jnp.zeros((bsz, groups, rep, p, n), x.dtype)
    _, y_off = lax.scan(step, state0, xs)
    return (y_diag + jnp.moveaxis(y_off, 0, 1)).reshape(bsz, seq, heads, p)

def even_mixer(u, w_in, conv_w, a_log, dt_bias, head_norm_w, w_out):
    bsz, seq, _ = u.shape
    proj = (u @ w_in).astype(jnp.float32)
    cuts = [int(c) for c in np.cumsum([A_WIDTH, A_WIDTH, A_WIDTH, 3 * B_WIDTH, B_WIDTH, B_HEADS])]
    qa, ka, va, qkv_b, z, beta_raw, a_raw = jnp.split(proj, cuts, axis=-1)
    qa, ka, va = (t.reshape(bsz, seq, A_HEADS, A_HEAD_DIM) for t in (qa, ka, va))
    o_a = dilated_window_attention(qa, ka, va)
    qkv_b = jax.nn.silu(causal_dwconv(qkv_b, conv_w))
    qb, kb, vb = (t.reshape(bsz, seq, B_HEADS, B_HEAD_DIM) for t in jnp.split(qkv_b, 3, axis=-1))
    beta = jax.nn.sigmoid(beta_raw)
    g = -jnp.exp(a_log) * jax.nn.softplus(a_raw + dt_bias)
    o_b = gated_delta_rule(l2norm(qb), l2norm(kb), vb, g, beta)
    o_b = rmsnorm(o_b, head_norm_w) * jax.nn.silu(z.reshape(bsz, seq, B_HEADS, B_HEAD_DIM))
    o = jnp.concatenate([o_a.reshape(bsz, seq, A_WIDTH), o_b.reshape(bsz, seq, B_WIDTH)], axis=-1)
    return (o @ w_out).astype(u.dtype)

def odd_mixer(u, w_in, conv_w, conv_b, dt_bias, a_log, d_skip, out_norm_w, w_out):
    bsz, seq, _ = u.shape
    proj = (u @ w_in).astype(jnp.float32)
    z, xbc, dt = jnp.split(proj, [C_D_INNER, C_D_INNER + C_XBC], axis=-1)
    xbc = jax.nn.silu(causal_dwconv(xbc, conv_w) + conv_b)
    xs, b_in, c_in = jnp.split(xbc, [C_D_INNER, C_D_INNER + C_GROUPS * C_STATE], axis=-1)
    xs = xs.reshape(bsz, seq, C_HEADS, C_HEAD_DIM)
    b_in = b_in.reshape(bsz, seq, C_GROUPS, C_STATE)
    c_in = c_in.reshape(bsz, seq, C_GROUPS, C_STATE)
    dt = jax.nn.softplus(dt + dt_bias)
    a = -jnp.exp(a_log) * dt
    y = ssd_chunked_scan(xs * dt[..., None], a, b_in, c_in) + d_skip[:, None] * xs
    y = y.reshape(bsz, seq, C_D_INNER) * jax.nn.silu(z)
    y = rmsnorm(y.reshape(bsz, seq, C_GROUPS, C_D_INNER // C_GROUPS), out_norm_w.reshape(C_GROUPS, -1))
    return (y.reshape(bsz, seq, C_D_INNER) @ w_out).astype(u.dtype)

def _dt_bias(key, shape):
    dt = jnp.exp(jax.random.uniform(key, shape, jnp.float32, math.log(1e-3), math.log(1e-1)))
    return dt + jnp.log(-jnp.expm1(-dt))

def first_inputs(seed: int = 0) -> dict:
    key = jax.random.key(seed)
    ks = iter(jax.random.split(key, 24))

    def nrm(shape, scale):
        return scale * jax.random.normal(next(ks), shape, jnp.float32)

    x = nrm((BATCH, SEQ, D_MODEL), 1.0)
    norm_w = 1.0 + nrm((DEPTH, 6, D_MODEL), 0.05)
    ffn_w_gate = nrm((DEPTH, 2, D_MODEL, D_FF), D_MODEL ** -0.5)
    ffn_w_up = nrm((DEPTH, 2, D_MODEL, D_FF), D_MODEL ** -0.5)
    ffn_w_down = nrm((DEPTH, 2, D_FF, D_MODEL), D_FF ** -0.5)
    even_w_in = nrm((N_EVEN, D_MODEL, EVEN_IN), D_MODEL ** -0.5)
    even_conv_w = nrm((N_EVEN, B_CONV, 3 * B_WIDTH), B_CONV ** -0.5)
    even_a_log = jnp.log(jax.random.uniform(next(ks), (N_EVEN, B_HEADS), jnp.float32, 1.0, 16.0))
    even_dt_bias = _dt_bias(next(ks), (N_EVEN, B_HEADS))
    even_head_norm_w = 1.0 + nrm((N_EVEN, B_HEAD_DIM), 0.05)
    even_w_out = nrm((N_EVEN, A_WIDTH + B_WIDTH, D_MODEL), (A_WIDTH + B_WIDTH) ** -0.5)
    odd_w_in = nrm((N_ODD, D_MODEL, ODD_IN), D_MODEL ** -0.5)
    odd_conv_w = nrm((N_ODD, C_CONV, C_XBC), C_CONV ** -0.5)
    odd_conv_b = nrm((N_ODD, C_XBC), 0.02)
    odd_dt_bias = _dt_bias(next(ks), (N_ODD, C_HEADS))
    odd_a_log = jnp.log(jax.random.uniform(next(ks), (N_ODD, C_HEADS), jnp.float32, 1.0, 16.0))
    odd_d_skip = 1.0 + nrm((N_ODD, C_HEADS), 0.05)
    odd_out_norm_w = 1.0 + nrm((N_ODD, C_D_INNER), 0.05)
    odd_w_out = nrm((N_ODD, C_D_INNER, D_MODEL), C_D_INNER ** -0.5)
    return {'x': x, 'norm_w': norm_w, 'ffn_w_gate': ffn_w_gate, 'ffn_w_up': ffn_w_up,
            'ffn_w_down': ffn_w_down, 'even_w_in': even_w_in, 'even_conv_w': even_conv_w,
            'even_a_log': even_a_log, 'even_dt_bias': even_dt_bias, 'even_head_norm_w': even_head_norm_w,
            'even_w_out': even_w_out, 'odd_w_in': odd_w_in, 'odd_conv_w': odd_conv_w,
            'odd_conv_b': odd_conv_b, 'odd_dt_bias': odd_dt_bias, 'odd_a_log': odd_a_log,
            'odd_d_skip': odd_d_skip, 'odd_out_norm_w': odd_out_norm_w, 'odd_w_out': odd_w_out}

def first_block(x, norm_w, ffn_w_gate, ffn_w_up, ffn_w_down, even_w_in, even_conv_w, even_a_log,
              even_dt_bias, even_head_norm_w, even_w_out, odd_w_in, odd_conv_w, odd_conv_b, odd_dt_bias,
              odd_a_log, odd_d_skip, odd_out_norm_w, odd_w_out):
    h = x
    for layer in range(DEPTH):
        nw = norm_w[layer]
        i = layer // 2
        f = swiglu(rmsnorm(h, nw[0]), ffn_w_gate[layer, 0], ffn_w_up[layer, 0], ffn_w_down[layer, 0])
        h = h + FFN_RES_SCALE * rmsnorm(f, nw[1])
        u = rmsnorm(h, nw[2])
        if layer % 2 == 0:
            m = even_mixer(u, even_w_in[i], even_conv_w[i], even_a_log[i], even_dt_bias[i],
                           even_head_norm_w[i], even_w_out[i])
        else:
            m = odd_mixer(u, odd_w_in[i], odd_conv_w[i], odd_conv_b[i], odd_dt_bias[i], odd_a_log[i],
                          odd_d_skip[i], odd_out_norm_w[i], odd_w_out[i])
        h = h + rmsnorm(m, nw[3])
        f = swiglu(rmsnorm(h, nw[4]), ffn_w_gate[layer, 1], ffn_w_up[layer, 1], ffn_w_down[layer, 1])
        h = h + FFN_RES_SCALE * rmsnorm(f, nw[5])
    return h


CTX_LEN = 256
GRID_W = 64
N_MIXERS = 3
DA_HEADS = 8
DA_HEAD_DIM = 64
DA_V_DIM = 2 * DA_HEAD_DIM
ROPE_F = DA_HEAD_DIM // 4
ROPE_THETA = 10000.0
Q_BLOCK = 128
FN_GROUPS = 8
FN_GROUP_DIM = D_MODEL // FN_GROUPS
HY_ORDER = 2
HY_EMB = 33
HY_BANDS = (HY_EMB - 1) // 2
HY_FILTER_HIDDEN = 64
HY_SIN_FREQ = 1.0
HY_FAST_DECAY = 0.3
HY_SLOW_DECAY = 1.5
HY_TARGET = 1e-2
HY_MAX_DECAY = math.log(HY_TARGET) / HY_FAST_DECAY
HY_MIN_DECAY = math.log(HY_TARGET) / HY_SLOW_DECAY
D_FF_2 = 3584
N_EXPERTS = 8
TOP_K = 2
MOE_BLOCK = 128
EPS = 1e-6


def rms_norm(x, g):
    xf = x.astype(jnp.float32)
    y = xf * lax.rsqrt(jnp.mean(xf * xf, axis=-1, keepdims=True) + EPS)
    return (y * g.astype(jnp.float32)).astype(x.dtype)

def axial_rope(x, cos, sin):
    xr = x.reshape(x.shape[:-1] + (2, 2, ROPE_F))
    cs = cos[None, :, None, None].astype(x.dtype)
    sn = sin[None, :, None, None].astype(x.dtype)
    x1, x2 = xr[..., 0, :], xr[..., 1, :]
    out = jnp.stack([x1 * cs - x2 * sn, x2 * cs + x1 * sn], axis=-2)
    return out.reshape(x.shape)

def diff_attention(h_l, h_c, cos, sin, w_qkv, lq1, lk1, lq2, lk2, subln_g, w_o, lam_init, with_ctx):
    B, L, D = h_l.shape

    def project(h):
        n = h.shape[1]
        q, k, v = jnp.split(h @ w_qkv, 3, axis=-1)
        return (q.reshape(B, n, DA_HEADS, 2, DA_HEAD_DIM),
                k.reshape(B, n, DA_HEADS, 2, DA_HEAD_DIM),
                v.reshape(B, n, DA_HEADS, DA_V_DIM))

    q_l, k_l, v_l = project(h_l)
    q_c, k_c, v_c = project(h_c)
    q_l = axial_rope(q_l, cos, sin)
    k_l = axial_rope(k_l, cos, sin)
    f32 = jnp.float32
    lam = (jnp.exp(jnp.sum(lq1.astype(f32) * lk1.astype(f32)))
           - jnp.exp(jnp.sum(lq2.astype(f32) * lk2.astype(f32))) + lam_init)
    scale = DA_HEAD_DIM ** -0.5

    def attend(q, k, v):
        n = q.shape[1]
        s = jnp.einsum('bqhnd,bkhnd->bnhqk', q, k).astype(f32) * scale
        p = jax.nn.softmax(s, axis=-1)
        a = (p[:, 0] - lam * p[:, 1]).astype(v.dtype)
        o = jnp.einsum('bhqk,bkhe->bqhe', a, v)
        o = rms_norm(o, subln_g) * (1.0 - lam_init)
        return o.reshape(B, n, DA_HEADS * DA_V_DIM)

    k_all = jnp.concatenate([k_c, k_l], axis=1)
    v_all = jnp.concatenate([v_c, v_l], axis=1)
    qb = q_l.reshape(B, L // Q_BLOCK, Q_BLOCK, DA_HEADS, 2, DA_HEAD_DIM).swapaxes(0, 1)
    o_l = lax.map(lambda q: attend(q, k_all, v_all), qb)
    y_l = o_l.swapaxes(0, 1).reshape(B, L, -1) @ w_o
    y_c = attend(q_c, k_c, v_c) @ w_o if with_ctx else None
    return y_l, y_c

def fourier_mix(h, w_o, b_o):
    B, L, D = h.shape
    hg = h.astype(jnp.float32).reshape(B, L, FN_GROUPS, FN_GROUP_DIM)
    f = jnp.fft.fftn(hg, axes=(1, 3), norm='ortho').real
    return f.reshape(B, L, D).astype(h.dtype) @ w_o + b_o

def short_conv(u, w, b):
    up = jnp.pad(u, ((0, 0), (1, 1), (0, 0)))
    return up[:, :-2] * w[0] + up[:, 1:-1] * w[1] + up[:, 2:] * w[2] + b

def hyena_filters(L, f_w1, f_b1, f_w2, f_b2, f_w3):
    f32 = jnp.float32
    D = f_w3.shape[-1] // (2 * HY_ORDER)
    t01 = jnp.linspace(0.0, 1.0, L, dtype=f32)[:, None]
    w = 2.0 * math.pi * jnp.arange(L, dtype=f32) / L
    bands = jnp.linspace(1e-4, HY_BANDS - 1, HY_BANDS, dtype=f32)
    fw = w[:, None] * bands[None, :]
    emb = jnp.concatenate([t01, jnp.cos(fw), -jnp.sin(fw)], axis=-1)
    hdn = jnp.sin(HY_SIN_FREQ * (emb @ f_w1.astype(f32) + f_b1.astype(f32)))
    hdn = jnp.sin(HY_SIN_FREQ * (hdn @ f_w2.astype(f32) + f_b2.astype(f32)))
    filt = (hdn @ f_w3.astype(f32)).reshape(L, HY_ORDER, 2, D)
    deltas = jnp.abs(jnp.linspace(HY_MIN_DECAY, HY_MAX_DECAY, D, dtype=f32))
    decay = jnp.exp(-t01 * deltas[None, :])
    filt = filt * decay[:, None, None, :]
    fwd, bwd = filt[:, :, 0], filt[:, :, 1]
    two = jnp.concatenate([fwd, jnp.zeros((1, HY_ORDER, D), f32), bwd[1:][::-1]], axis=0)
    return jnp.fft.rfft(two, axis=0)

def hyena_mixer(h, w_in, conv_w, conv_b, f_w1, f_b1, f_w2, f_b2, f_w3, f_bias, w_o):
    L = h.shape[1]
    u = short_conv(h @ w_in, conv_w, conv_b)
    x1, x2, v = jnp.split(u, 3, axis=-1)
    kf = hyena_filters(L, f_w1, f_b1, f_w2, f_b2, f_w3)
    z = v
    for n, gate in enumerate((x1, x2)):
        zf = jnp.fft.rfft(z.astype(jnp.float32), n=2 * L, axis=1)
        y = jnp.fft.irfft(zf * kf[None, :, n], n=2 * L, axis=1)[:, :L]
        z = gate * (y.astype(h.dtype) + f_bias[n] * z)
    return z @ w_o

def swiglu_2(h, w1, w3, w2):
    return (jax.nn.silu(h @ w1) * (h @ w3)) @ w2

def moe_swiglu(h, router, w1, w3, w2):
    T, D = h.shape
    logits = (h @ router).astype(jnp.float32)
    top_v, top_i = lax.top_k(logits, TOP_K)
    gates = jax.nn.softmax(top_v, axis=-1).astype(h.dtype)
    flat_e = top_i.reshape(-1)
    flat_w = gates.reshape(-1)
    flat_tok = jnp.repeat(jnp.arange(T, dtype=jnp.int32), TOP_K)
    TK = T * TOP_K
    counts = jnp.bincount(flat_e, length=N_EXPERTS)
    padded = (counts + MOE_BLOCK - 1) // MOE_BLOCK * MOE_BLOCK
    pad_start = jnp.cumsum(padded) - padded
    start = jnp.cumsum(counts) - counts
    order = jnp.argsort(flat_e)
    se = flat_e[order]
    dest = pad_start[se] + jnp.arange(TK, dtype=jnp.int32) - start[se]
    n_blocks = -(-TK // MOE_BLOCK) + N_EXPERTS
    n_rows = n_blocks * MOE_BLOCK
    row_tok = jnp.full((n_rows,), T, jnp.int32).at[dest].set(flat_tok[order])
    row_w = jnp.zeros((n_rows,), h.dtype).at[dest].set(flat_w[order])
    block_start = jnp.arange(n_blocks, dtype=jnp.int32) * MOE_BLOCK
    block_e = jnp.minimum(jnp.searchsorted(jnp.cumsum(padded), block_start, side='right'), N_EXPERTS - 1)
    h_ext = jnp.concatenate([h, jnp.zeros((1, D), h.dtype)], axis=0)
    xb = h_ext[row_tok].reshape(n_blocks, MOE_BLOCK, D)

    def expert_block(args):
        xe, e = args
        return swiglu_2(xe, w1[e], w3[e], w2[e])

    yb = lax.map(expert_block, (xb, block_e))
    y = jnp.zeros((T + 1, D), h.dtype).at[row_tok].add(yb.reshape(n_rows, D) * row_w[:, None])
    return y[:T]

def second_inputs(seed: int = 0) -> dict:
    key = jax.random.key(seed)
    ks = iter(jax.random.split(key, 64))
    D = D_MODEL

    def nrm(shape, s):
        return jax.random.normal(next(ks), shape, jnp.float32) * s

    n_a = len(range(0, DEPTH, N_MIXERS))
    n_b = len(range(1, DEPTH, N_MIXERS))
    n_c = len(range(2, DEPTH, N_MIXERS))
    n_dense = len(range(0, DEPTH, 2))
    n_moe = len(range(1, DEPTH, 2))
    return {
        'x': nrm((BATCH, SEQ, D), 1.0),
        'c': nrm((BATCH, D), 1.0),
        'ctx': nrm((BATCH, CTX_LEN, D), 1.0),
        'c_ctx': nrm((D,), 1.0),
        'ada_w': nrm((DEPTH, D, 6 * D), 0.5 * D ** -0.5),
        'ada_b': nrm((DEPTH, 6 * D), 0.02),
        'norm1_g': 1.0 + nrm((DEPTH, D), 0.02),
        'norm2_g': 1.0 + nrm((DEPTH, D), 0.02),
        'attn_w_qkv': nrm((n_a, D, 3 * D), D ** -0.5),
        'attn_lq1': nrm((n_a, DA_HEAD_DIM), 0.1),
        'attn_lk1': nrm((n_a, DA_HEAD_DIM), 0.1),
        'attn_lq2': nrm((n_a, DA_HEAD_DIM), 0.1),
        'attn_lk2': nrm((n_a, DA_HEAD_DIM), 0.1),
        'attn_subln_g': 1.0 + nrm((n_a, DA_V_DIM), 0.02),
        'attn_w_o': nrm((n_a, D, D), D ** -0.5),
        'fnet_w_o': nrm((n_b, D, D), D ** -0.5),
        'fnet_b_o': nrm((n_b, D), 0.02),
        'hy_w_in': nrm((n_c, D, 3 * D), D ** -0.5),
        'hy_conv_w': nrm((n_c, 3, 3 * D), 0.5),
        'hy_conv_b': nrm((n_c, 3 * D), 0.02),
        'hy_f_w1': nrm((n_c, HY_EMB, HY_FILTER_HIDDEN), HY_EMB ** -0.5),
        'hy_f_b1': nrm((n_c, HY_FILTER_HIDDEN), 0.1),
        'hy_f_w2': nrm((n_c, HY_FILTER_HIDDEN, HY_FILTER_HIDDEN), HY_FILTER_HIDDEN ** -0.5),
        'hy_f_b2': nrm((n_c, HY_FILTER_HIDDEN), 0.1),
        'hy_f_w3': nrm((n_c, HY_FILTER_HIDDEN, HY_ORDER * 2 * D), 0.2 * HY_FILTER_HIDDEN ** -0.5),
        'hy_f_bias': nrm((n_c, HY_ORDER, D), 0.5),
        'hy_w_o': nrm((n_c, D, D), D ** -0.5),
        'ff_w1': nrm((n_dense, D, D_FF_2), D ** -0.5),
        'ff_w3': nrm((n_dense, D, D_FF_2), D ** -0.5),
        'ff_w2': nrm((n_dense, D_FF_2, D), D_FF_2 ** -0.5),
        'moe_router': nrm((n_moe, D, N_EXPERTS), D ** -0.5),
        'moe_w1': nrm((n_moe, N_EXPERTS, D, D_FF_2), D ** -0.5),
        'moe_w3': nrm((n_moe, N_EXPERTS, D, D_FF_2), D ** -0.5),
        'moe_w2': nrm((n_moe, N_EXPERTS, D_FF_2, D), D_FF_2 ** -0.5),
        'final_g': 1.0 + nrm((D,), 0.02),
    }

def second_block(x, c, ctx, c_ctx, ada_w, ada_b, norm1_g, norm2_g,
              attn_w_qkv, attn_lq1, attn_lk1, attn_lq2, attn_lk2, attn_subln_g, attn_w_o,
              fnet_w_o, fnet_b_o,
              hy_w_in, hy_conv_w, hy_conv_b, hy_f_w1, hy_f_b1, hy_f_w2, hy_f_b2, hy_f_w3, hy_f_bias, hy_w_o,
              ff_w1, ff_w3, ff_w2, moe_router, moe_w1, moe_w3, moe_w2, final_g):
    B, L, D = x.shape
    f32 = jnp.float32
    grid_rows = L // GRID_W
    row = jnp.repeat(jnp.arange(grid_rows, dtype=f32), GRID_W)
    col = jnp.tile(jnp.arange(GRID_W, dtype=f32), grid_rows)
    freqs = ROPE_THETA ** (-jnp.arange(ROPE_F, dtype=f32) / ROPE_F)
    ang = jnp.stack([row[:, None] * freqs, col[:, None] * freqs], axis=1)
    cos, sin = jnp.cos(ang), jnp.sin(ang)
    silu_c = jax.nn.silu(c)
    silu_cc = jax.nn.silu(c_ctx)

    for i in range(DEPTH):
        last = i == DEPTH - 1
        kind, j = i % N_MIXERS, i // N_MIXERS
        mod_l = (silu_c @ ada_w[i] + ada_b[i])[:, None, :]
        mod_c = silu_cc @ ada_w[i] + ada_b[i]
        sh1_l, sc1_l, g1_l, sh2_l, sc2_l, g2_l = jnp.split(mod_l, 6, axis=-1)
        sh1_c, sc1_c, g1_c, sh2_c, sc2_c, g2_c = jnp.split(mod_c, 6, axis=-1)

        h_l = rms_norm(x, norm1_g[i]) * (1.0 + sc1_l) + sh1_l
        h_c = rms_norm(ctx, norm1_g[i]) * (1.0 + sc1_c) + sh1_c
        if kind == 0:
            y_l, y_c = diff_attention(h_l, h_c, cos, sin, attn_w_qkv[j], attn_lq1[j], attn_lk1[j],
                                      attn_lq2[j], attn_lk2[j], attn_subln_g[j], attn_w_o[j],
                                      0.8 - 0.6 * math.exp(-0.3 * i), not last)
        elif kind == 1:
            y_l = fourier_mix(h_l, fnet_w_o[j], fnet_b_o[j])
            y_c = None if last else fourier_mix(h_c, fnet_w_o[j], fnet_b_o[j])
        else:
            hp = (hy_w_in[j], hy_conv_w[j], hy_conv_b[j], hy_f_w1[j], hy_f_b1[j], hy_f_w2[j],
                  hy_f_b2[j], hy_f_w3[j], hy_f_bias[j], hy_w_o[j])
            y_l = hyena_mixer(h_l, *hp)
            y_c = None if last else hyena_mixer(h_c, *hp)
        x = x + g1_l * y_l
        if not last:
            ctx = ctx + g1_c * y_c

        h2_l = (rms_norm(x, norm2_g[i]) * (1.0 + sc2_l) + sh2_l).reshape(B * L, D)
        if last:
            tokens = h2_l
        else:
            h2_c = (rms_norm(ctx, norm2_g[i]) * (1.0 + sc2_c) + sh2_c).reshape(-1, D)
            tokens = jnp.concatenate([h2_l, h2_c], axis=0)
        if i % 2 == 0:
            k = i // 2
            f = swiglu_2(tokens, ff_w1[k], ff_w3[k], ff_w2[k])
        else:
            k = i // 2
            f = moe_swiglu(tokens, moe_router[k], moe_w1[k], moe_w3[k], moe_w2[k])
        x = x + g2_l * f[:B * L].reshape(B, L, D)
        if not last:
            ctx = ctx + g2_c * f[B * L:].reshape(B, -1, D)

    return rms_norm(x, final_g)


def setup_inputs(seed=0):
    out = dict(first_inputs(seed))
    for name, value in second_inputs(seed + 1).items():
        if name != "x":
            out[name + "_2"] = value
    return out


def reference(
    x, norm_w, ffn_w_gate, ffn_w_up, ffn_w_down, even_w_in, even_conv_w, even_a_log,
    even_dt_bias, even_head_norm_w, even_w_out, odd_w_in, odd_conv_w, odd_conv_b, odd_dt_bias,
    odd_a_log, odd_d_skip, odd_out_norm_w, odd_w_out, c_2, ctx_2, c_ctx_2, ada_w_2, ada_b_2,
    norm1_g_2, norm2_g_2, attn_w_qkv_2, attn_lq1_2, attn_lk1_2, attn_lq2_2, attn_lk2_2,
    attn_subln_g_2, attn_w_o_2, fnet_w_o_2, fnet_b_o_2, hy_w_in_2, hy_conv_w_2, hy_conv_b_2,
    hy_f_w1_2, hy_f_b1_2, hy_f_w2_2, hy_f_b2_2, hy_f_w3_2, hy_f_bias_2, hy_w_o_2, ff_w1_2,
    ff_w3_2, ff_w2_2, moe_router_2, moe_w1_2, moe_w3_2, moe_w2_2, final_g_2,
):
    x = first_block(
        x, norm_w, ffn_w_gate, ffn_w_up, ffn_w_down, even_w_in, even_conv_w, even_a_log,
        even_dt_bias, even_head_norm_w, even_w_out, odd_w_in, odd_conv_w, odd_conv_b,
        odd_dt_bias, odd_a_log, odd_d_skip, odd_out_norm_w, odd_w_out,
    )
    return second_block(
        x, c_2, ctx_2, c_ctx_2, ada_w_2, ada_b_2, norm1_g_2, norm2_g_2, attn_w_qkv_2,
        attn_lq1_2, attn_lk1_2, attn_lq2_2, attn_lk2_2, attn_subln_g_2, attn_w_o_2, fnet_w_o_2,
        fnet_b_o_2, hy_w_in_2, hy_conv_w_2, hy_conv_b_2, hy_f_w1_2, hy_f_b1_2, hy_f_w2_2,
        hy_f_b2_2, hy_f_w3_2, hy_f_bias_2, hy_w_o_2, ff_w1_2, ff_w3_2, ff_w2_2, moe_router_2,
        moe_w1_2, moe_w3_2, moe_w2_2, final_g_2,
    )


_drawn_inputs = setup_inputs


def setup_inputs(seed=0):
    import zlib

    import numpy as np

    out = dict(_drawn_inputs(seed))
    spreads = {}
    factors = {'odd_conv_b': 3.726,
     'ada_b_2': 2.765,
     'norm1_g_2': 8.0,
     'norm2_g_2': 7.253,
     'attn_lq1_2': 64.0,
     'attn_lk1_2': 64.0,
     'attn_lq2_2': 5.387,
     'attn_lk2_2': 4.903,
     'attn_subln_g_2': 8.0,
     'fnet_b_o_2': 59.048,
     'final_g_2': 8.131}
    for name, (base, spread) in spreads.items():
        noise = np.random.default_rng([zlib.crc32(name.encode()), seed]).standard_normal(out[name].shape)
        drawn = base * np.exp(spread * noise) if base else spread * noise
        out[name] = jnp.asarray(drawn.astype(out[name].dtype))
    for name, factor in factors.items():
        out[name] = (out[name] * factor).astype(out[name].dtype)
    return out
```

```python
from contextlib import ExitStack

import concourse.bass as bass
from concourse import mybir

F32 = mybir.dt.float32
F32R = mybir.dt.float32r
I32 = mybir.dt.int32
U32 = mybir.dt.uint32
ALU = mybir.AluOpType
ACT = mybir.ActivationFunctionType
AX_X = mybir.AxisListType.X

P = 128
TOKENS = 256
TB = TOKENS // P
DM = 1024
DC = DM // P
BANK = 512
FF1, FF2 = 2816, 3584
EPS = 1e-6
NEG = -1e30

RING = 7
SLOT = 2048
GRAN = SLOT // 2
SPLITS = 4

A_HEADS, A_DIM = 8, 64
B_HEADS, B_DIM = 4, 128
EVEN_IN = 3592
CONV_K = 4
C_HEADS, C_DIM, C_GROUPS = 32, 64, 4
C_INNER = C_HEADS * C_DIM
C_REP = C_HEADS // C_GROUPS
ODD_IN = 5152
DA_HEADS, DA_DIM = 8, 64
LAM_INIT = 0.2
N_EXPERTS = 8
MOE_SLOTS = 3 * DM * FF2 // (P * SLOT)
MAX_EXTRA = 3

C_IDENT, C_ONES, C_TRI, C_STRICT, C_NEG = 0, 128, 256, 384, 512
C_CORE = 640
C_LEV = 640
C_ATTN = C_LEV + 7 * P
C_ROPE = C_ATTN + 384
C_DFTG = C_ROPE + 128
C_DFTL = C_DFTG + 256
C_IOTA = C_DFTL + 1024
C_ALL = C_IOTA + 136

V_ECONV, V_OCB, V_OON, V_SUBLN, V_C, V_CTX, V_FIN, V_FNB, V_HNW = 0, 48, 72, 88, 89, 97, 105, 113, 121
ROWS_A = 122
V_OCONV = P
V_NW = 2 * P
V_N1 = V_NW + 96
V_N2 = V_N1 + 16
V_ADAB = 3 * P


class Count:

    def __init__(self):
        self.at = {}
        self.block = None
        self.per = {}

    def __call__(self, sem, k=1):
        self.at[sem.name] = self.at.get(sem.name, 0) + k
        return self.last(sem)

    def gran(self, v):
        return v if self.block is None else v + self.block * (2 * MOE_SLOTS)

    def ring(self, v):
        return v if self.block is None else v + self.block * (16 * MOE_SLOTS // RING)

    def last(self, sem, back=0):
        v = self.at.get(sem.name, 0) - back
        return v if self.block is None else v + self.block * self.per[sem.name]


def bc(ap, m):
    return ap.unsqueeze(len(ap.shape)).to_broadcast(list(ap.shape) + [m])


def bc_mid(ap, m):
    return ap.unsqueeze(1).to_broadcast([ap.shape[0], m, ap.shape[1]])


def host_constants():
    import numpy as np
    out = np.zeros((P, C_ALL), np.float32)
    p = np.arange(P)
    i, j = p[:, None], p[None, :]
    out[:, C_IDENT:C_IDENT + P] = i == j
    out[:, C_ONES:C_ONES + P] = 1
    out[:, C_TRI:C_TRI + P] = i <= j
    out[:, C_STRICT:C_STRICT + P] = i < j
    out[:, C_NEG:C_NEG + P] = np.where(j < i, NEG, 0)
    for lev in range(7):
        s = 1 << lev
        out[:, C_LEV + lev * P:C_LEV + (lev + 1) * P] = (i // (2 * s) == j // (2 * s)) & (j % (2 * s) >= s) & (i % (2 * s) < s)
    for tb in range(TB):
        t = (tb * P + p)[:, None]
        s = np.arange((tb + 1) * P)[None, :]
        d = t - s
        count = ((d >= 0) & (d <= 128)).astype(int) + ((d >= 0) & (d % 4 == 0)) + ((d >= 0) & (d % 16 == 0))
        at = C_ATTN + tb * P
        out[:, at:at + (tb + 1) * P] = np.where(count > 0, np.log(np.maximum(count, 1)), NEG)
    freqs = np.float32(10000.0) ** (-np.arange(16, dtype=np.float32) / np.float32(16))
    for tb in range(TB):
        t = tb * P + p
        ang = np.stack([(t // 64)[:, None].astype(np.float32) * freqs, (t % 64)[:, None].astype(np.float32) * freqs], 1)
        out[:, C_ROPE + tb * 32:C_ROPE + tb * 32 + 32] = np.cos(ang).reshape(P, 32)
        out[:, C_ROPE + 64 + tb * 32:C_ROPE + 64 + tb * 32 + 32] = np.sin(ang).reshape(P, 32)
    w = 2 * np.pi * (i * j % P) / P
    out[:, C_DFTG:C_DFTG + P] = np.cos(w) / np.sqrt(P)
    out[:, C_DFTG + P:C_DFTG + 2 * P] = np.sin(w) / np.sqrt(P)
    for tb in range(TB):
        w = 2 * np.pi * ((tb * P + p)[:, None] * np.arange(TOKENS)[None, :] % TOKENS) / TOKENS
        out[:, C_DFTL + tb * TOKENS:C_DFTL + (tb + 1) * TOKENS] = np.cos(w) / np.sqrt(TOKENS)
        out[:, C_DFTL + 512 + tb * TOKENS:C_DFTL + 512 + (tb + 1) * TOKENS] = -np.sin(w) / np.sqrt(TOKENS)
    out[:, C_IOTA:C_IOTA + P] = j
    out[:, C_IOTA + P:C_IOTA + P + 8] = np.arange(8)
    return out


def build_block_kernel(nc, t, const, out):
    ctx = ExitStack()
    with ctx:
        def sb(name, shape, dt=F32):
            return ctx.enter_context(nc.sbuf_tensor(name, shape, dt))

        def sem(name):
            return ctx.enter_context(nc.semaphore(name))

        w_raw = sb("w_raw", [P, RING, SLOT])
        w_hi = sb("w_hi", [P, SPLITS, GRAN], F32R)
        w_lo = sb("w_lo", [P, SPLITS, GRAN], F32R)
        act_hi = sb("act_hi", [P, 16, TOKENS], F32R)
        act_lo = sb("act_lo", [P, 16, TOKENS], F32R)
        h = sb("h", [P, TB, DM])
        xn = sb("xn", [P, TB, DM])
        xt = sb("xt", [P, 2 * DM])
        sg = sb("sg", [P, 2 * BANK])
        hp = sb("hp", [P, 2 * BANK])
        wbc = sb("wbc", [P, DM])
        scr = sb("scr", [P, 12800])
        small = sb("small", [P, 768])
        cst = sb("cst", [P, C_CORE])
        lev = sb("lev", [P, 7, P])
        rope = sb("rope", [P, 2, TB, 32])
        iota = sb("iota", [P, P + 8])
        dtw = sb("dtw", [P, 12, 64])
        colv = sb("colv", [P, 3 * P + 96])
        ms = sb("ms", [P, 64])
        rt = sb("rt", [P, 64])
        rstd = sb("rstd", [P, 64])
        modt = sb("modt", [P, 64])
        eid = sb("eid", [1, 12], I32)
        ssq = sb("ssq", [P, 64])
        ps = ctx.enter_context(nc.psum_tensor("ps", [P, 8, BANK], F32))

        ident = cst[:, C_IDENT:C_IDENT + P]
        ones = cst[:, C_ONES:C_ONES + P]
        tri = cst[:, C_TRI:C_TRI + P]
        strict = cst[:, C_STRICT:C_STRICT + P]
        neg = cst[:, C_NEG:C_NEG + P]

        def banks(b, k=1):
            return ps[:, b:b + k, :].rearrange("p b n -> p (b n)")

        boot = sem("boot")
        w_landed = [sem(f"w_landed{i}") for i in range(RING)]
        hi_done = sem("hi_done")
        lo_done = sem("lo_done")
        gran_used = sem("gran_used")
        dve_link = sem("dve_link")
        act_link = sem("act_link")
        rows_t = sem("rows_t")
        h_ready = sem("h_ready")
        h_first = sem("h_first")
        sq_done = sem("sq_done")
        ms_done = sem("ms_done")
        rt_done = sem("rt_done")
        xn_done = sem("xn_done")
        tp_done = sem("tp_done")
        xt_done = sem("xt_done")
        ahi_done = sem("ahi_done")
        alo_done = sem("alo_done")
        silu_done = sem("silu_done")
        hid_done = sem("hid_done")
        hid_t = sem("hid_t")
        hid_x = sem("hid_x")
        hhi_done = sem("hhi_done")
        hlo_done = sem("hlo_done")
        diag_done = sem("diag_done")
        bc_ready = sem("bc_ready")

        proj_out = sem("proj_out")
        cv_tp = sem("cv_tp")
        cv_done = sem("cv_done")
        cv_act = sem("cv_act")
        qk_tp = sem("qk_tp")
        qk_cp = sem("qk_cp")
        at_sc = sem("at_sc")
        at_mx = sem("at_mx")
        at_p = sem("at_p")
        at_pt = sem("at_pt")
        at_pc = sem("at_pc")
        at_pv = sem("at_pv")
        at_o = sem("at_o")
        sv_in = sem("sv_in")
        sv_out = sem("sv_out")
        dl_g = sem("dl_g")
        dl_gc = sem("dl_gc")
        dl_tm = sem("dl_tm")
        dl_in = sem("dl_in")
        dl_t3 = sem("dl_t3")
        dl_tc = sem("dl_tc")
        dl_lg = sem("dl_lg")
        dl_R = sem("dl_R")
        dl_dt = sem("dl_dt")
        dl_at = sem("dl_at")
        dl_xt = sem("dl_xt")
        dl_xtt = sem("dl_xtt")
        dl_off = sem("dl_off")
        dl_x = sem("dl_x")
        dl_y = sem("dl_y")
        dl_yc = sem("dl_yc")
        dl_xy = sem("dl_xy")
        dl_u = sem("dl_u")
        dl_uc = sem("dl_uc")
        dl_ws = sem("dl_ws")
        dl_vn = sem("dl_vn")
        dl_o = sem("dl_o")

        o_tp = sem("o_tp")
        o_tc = sem("o_tc")
        og_x = sem("og_x")
        og_cb = sem("og_cb")
        og_cc = sem("og_cc")
        og_la = sem("og_la")
        og_R = sem("og_R")
        og_e = sem("og_e")
        og_m = sem("og_m")
        og_y = sem("og_y")
        og_s = sem("og_s")
        og_sc = sem("og_sc")
        og_off = sem("og_off")
        og_yz = sem("og_yz")

        ada_in = [sem(f"ada_in{i}") for i in range(2)]
        ada_sum = sem("ada_sum")
        ctx_in = sem("ctx_in")
        tab_in = sem("tab_in")
        ada_mul = sem("ada_mul")
        mod_col = sem("mod_col")
        rope_link = sem("rope_link")
        rope_done = sem("rope_done")
        da_qt = sem("da_qt")
        da_qc = sem("da_qc")
        da_kt = sem("da_kt")
        da_kc = sem("da_kc")
        da_s = sem("da_s")
        da_m = sem("da_m")
        da_e = sem("da_e")
        da_a = sem("da_a")
        da_at = sem("da_at")
        da_ac = sem("da_ac")
        da_o = sem("da_o")
        da_oc = sem("da_oc")
        ft_x = sem("ft_x")
        ft_c = sem("ft_c")
        mo_lg = sem("mo_lg")
        mo_ex = sem("mo_ex")
        mo_v = sem("mo_v")
        mo_sel = sem("mo_sel")
        mo_rank = sem("mo_rank")
        mo_ids = sem("mo_ids")
        row_read = sem("row_read")
        mo_link = sem("mo_link")
        mo_p = sem("mo_p")
        mo_x = sem("mo_x")
        mo_xc = sem("mo_xc")
        mo_xh = sem("mo_xh")
        mo_xl = sem("mo_xl")
        mo_pt = sem("mo_pt")
        mo_ptc = sem("mo_ptc")
        mo_y = sem("mo_y")
        mo_c = sem("mo_c")
        mo_cc = sem("mo_cc")
        mo_end = sem("mo_end")
        mo_end_y = sem("mo_end_y")
        mo_end_c = sem("mo_end_c")
        fin_link = sem("fin_link")
        fin = sem("fin")
        out_done = sem("out_done")

        slots = []

        def plan_up(w, n0, width):
            chunks = min(DC, SLOT // width)
            for k0 in range(0, w.shape[0], chunks * P):
                slots.append((w[k0:k0 + chunks * P, n0:n0 + width].rearrange("(c p) n -> p c n", p=P), chunks, width))

        def plan_down(w, k0, rows):
            for k in range(k0, k0 + rows, 2 * P):
                slots.append((w[k:k + 2 * P, :].rearrange("(c p) n -> p c n", p=P), 2, DM))

        def steps(ff):
            return [(f, min(BANK, ff - f)) for f in range(0, ff, BANK)]

        def plan_ff(wg, wu, wd, ff):
            s = steps(ff)
            for i, (f, width) in enumerate(s):
                plan_up(wg, f, width)
                plan_up(wu, f, width)
                if i:
                    plan_down(wd, *s[i - 1])
            plan_down(wd, *s[-1])

        def plan_proj(w, n):
            for n0 in range(0, n, BANK):
                plan_up(w, n0, min(BANK, n - n0))

        e_qkv = scr[:, 0:3072].rearrange("p (k b n) -> p k b n", k=3, b=TB)
        e_raw = scr[:, 3072:6144].rearrange("p (b n) -> p b n", b=TB)
        e_ba = scr[:, 6144:6160].rearrange("p (b n) -> p b n", b=TB)
        e_sz = scr[:, 6160:7184].rearrange("p (b n) -> p b n", b=TB)
        e_cv = scr[:, 7184:10256].rearrange("p (c n) -> p c n", c=12)
        e_qt = scr[:, 10256:11280].rearrange("p (c n) -> p c n", c=4)
        e_kt = scr[:, 11280:12304].rearrange("p (c n) -> p c n", c=4)
        e_mask = scr[:, 12304:12688]
        a_s = scr[:, 3072:3840].rearrange("p (i n) -> p i n", i=2)
        a_p = scr[:, 3840:4608].rearrange("p (i n) -> p i n", i=2)
        a_pt = scr[:, 4608:5376].rearrange("p (i n) -> p i n", i=2)
        d_tm = scr[:, 0:1536].rearrange("p (c n) -> p c n", c=12)
        d_kb, d_kbg, d_kd, d_qd, d_XT, d_X, d_Y, d_S, d_QK = [
            scr[:, 1536 + 512 * i:2048 + 512 * i].rearrange("p (c n) -> p c n", c=4) for i in range(9)]
        d_DT, d_A = [scr[:, 10256 + 512 * i:10768 + 512 * i].rearrange("p (c n) -> p c n", c=4) for i in range(2)]
        d_qT, d_kT, d_kbT, d_qdT = [xt[:, 512 * i:512 * i + 512].rearrange("p (c n) -> p c n", c=4) for i in range(4)]
        d_off = [d_tm[:, 0:4, :], d_kb]
        o_z = scr[:, 0:4096].rearrange("p (b n) -> p b n", b=TB)
        o_x = scr[:, 4096:8192].rearrange("p (b n) -> p b n", b=TB)
        o_bc = scr[:, 8192:10240].rearrange("p (c n) -> p c n", c=8)
        o_bt = scr[:, 10240:10752].rearrange("p (c n) -> p c n", c=4)
        o_xdt = scr[:, 10752:11776].rearrange("p (b n) -> p b n", b=TB)
        o_xd, o_st, = scr[:, 11776:12288], scr[:, 12288:12800]
        T_X, T_ABS, T_E, T_LN, T_DT, T_A, T_CUM, T_TOT, T_REST, T_EDEC, T_ECUM, T_NCUM = range(12)
        m_w = scr[:, 0:4096].rearrange("p (i c n) -> p i c n", i=2, c=2)
        m_sum = scr[:, 4096:10240]
        m_sumc = scr[:, 10240:12288]
        ctx_x = scr[:, 0:2048].rearrange("p (b n) -> p b n", b=TB)
        da_k = scr[:, 0:4096].rearrange("p (b n) -> p b n", b=4)
        da_kT = scr[:, 4096:8192].rearrange("p (c n) -> p c n", c=8)
        da_v = scr[:, 8192:12288].rearrange("p (b n) -> p b n", b=4)
        da_aT = scr[:, 0:1024].rearrange("p (i n) -> p i n", i=2)
        da_sq = scr[:, 1024:3072].rearrange("p (u n) -> p u n", u=16)

        def da_qT(c):
            return (sg if c < 4 else hp)[:, (c % 4) * TOKENS:(c % 4 + 1) * TOKENS]

        def f_z(g):
            at = 4096 + 512 * g if g < 6 else 11520 + 512 * (g - 6)
            return scr[:, at:at + 512].rearrange("p (b n) -> p b n", b=TB)

        f_g = scr[:, 10240:10496]
        f_l = scr[:, 10496:11520].rearrange("p (k b n) -> p k b n", k=2, b=TB)
        mo_acc = scr[:, 0:2048].rearrange("p (b n) -> p b n", b=TB)
        mo_ye = scr[:, 2048:3072]
        mo_P = scr[:, 3072:3328].rearrange("p (b n) -> p b n", b=TB)
        mo_PG = scr[:, 3328:3584].rearrange("p (b n) -> p b n", b=TB)
        mo_PT = scr[:, 3584:3840].rearrange("p (b n) -> p b n", b=TB)
        fin_g = scr[:, 4096:5120]
        dt_flat = dtw[:].rearrange("p a n -> p (a n)")
        modv, modc = modt[:, 0:48], modt[:, 48:64]
        MOD_B1, MOD_A1, MOD_G1, MOD_B2, MOD_A2, MOD_G2 = range(0, 48, 8)
        r_w = dt_flat[:, 64:128].rearrange("p (c e) -> p c e", c=DC)
        r_lg, r_tmp, r_oh1, r_oh2 = [dt_flat[:, 128 + 16 * i:144 + 16 * i].rearrange("p (b e) -> p b e", b=TB) for i in range(4)]
        r_v1, r_v2, r_g1, r_g2, r_d, r_e = [dt_flat[:, 192 + 2 * i:194 + 2 * i] for i in range(6)]
        R_RANK, R_SEL, R_GATE = 0, 2, 4
        r_q = dt_flat[:, 256:304].rearrange("p (q e) -> p q e", q=6)
        r_cnt, r_code, r_rev = [dt_flat[:, 304 + 8 * i:312 + 8 * i] for i in range(3)]
        r_ck = dt_flat[:, 328:331]
        r_ohk = dt_flat[:, 336:360].rearrange("p (k e) -> p k e", k=3)
        r_t48 = dt_flat[:, 360:408].rearrange("p (q e) -> p q e", q=6)
        r_tab = dt_flat[:, 408:480].rearrange("p (q b) -> p q b", q=6)
        r_ids = dt_flat[:, 480:492]
        silc = small[:, 360:376]
        m_alog4, m_dtb4 = small[:, 0:4], small[:, 4:8]
        m_dtb, m_alog, m_dskip = small[:, 8:40], small[:, 40:72], small[:, 72:104]
        m_lq = small[:, 104:360].rearrange("p (k n) -> p k n", k=4)
        work = small[:, 384:768]

        def w8(i, n=8):
            return work[:, 8 * i:8 * i + n]

        for l in range(1):
            plan_ff(t["ffn_w_gate"][l, 0], t["ffn_w_up"][l, 0], t["ffn_w_down"][l, 0], FF1)
        plan_proj(t["even_w_in"][0], EVEN_IN)
        plan_down(t["even_w_out"][0], 0, DM)
        plan_ff(t["ffn_w_gate"][0, 1], t["ffn_w_up"][0, 1], t["ffn_w_down"][0, 1], FF1)
        plan_ff(t["ffn_w_gate"][1, 0], t["ffn_w_up"][1, 0], t["ffn_w_down"][1, 0], FF1)
        plan_proj(t["odd_w_in"][0], ODD_IN)
        plan_down(t["odd_w_out"][0], 0, C_INNER)
        plan_ff(t["ffn_w_gate"][1, 1], t["ffn_w_up"][1, 1], t["ffn_w_down"][1, 1], FF1)
        plan_proj(t["attn_w_qkv_2"][0], 3 * DM)
        plan_down(t["attn_w_o_2"][0], 0, DM)
        plan_ff(t["ff_w1_2"][0], t["ff_w3_2"][0], t["ff_w2_2"][0], FF2)
        plan_down(t["fnet_w_o_2"][0], 0, DM)
        moe_from = len(slots)
        plan_ff(t["moe_w1_2"][0, 0], t["moe_w3_2"][0, 0], t["moe_w2_2"][0, 0], FF2)
        n_slots = len(slots)

        block = ctx.enter_context(nc.Block())

        @block.sync
        def _(sp):
            n = Count()
            boots = [
                (h[:], t["x"][0].rearrange("(b p) n -> p b n", p=P)),
                (cst[:], const[:, 0:C_CORE]),
                (scr[0:48, 0:P], t["even_conv_w"][0].rearrange("k (c p) -> (k c) p", p=P)),
                (scr[48:72, 0:P], t["odd_conv_b"][0].rearrange("(c p) -> c p", p=P)),
                (scr[72:88, 0:P], t["odd_out_norm_w"][0].rearrange("(c p) -> c p", p=P)),
                (scr[88:89, 0:P], t["attn_subln_g_2"]),
                (scr[89:97, 0:P], t["c_2"].rearrange("a (c p) -> (a c) p", p=P)),
                (scr[97:105, 0:P], t["c_ctx_2"].rearrange("(c p) -> c p", p=P)),
                (scr[105:113, 0:P], t["final_g_2"].rearrange("(c p) -> c p", p=P)),
                (scr[113:121, 0:P], t["fnet_b_o_2"][0].rearrange("(c p) -> c p", p=P)),
                (scr[121:122, 0:P], t["even_head_norm_w"]),
                (scr[0:96, P:2 * P], t["odd_conv_w"][0].rearrange("k (c p) -> (k c) p", p=P)),
                (scr[0:96, 2 * P:3 * P], t["norm_w"].rearrange("l j (c p) -> (l j c) p", p=P)),
                (scr[96:112, 2 * P:3 * P], t["norm1_g_2"].rearrange("l (c p) -> (l c) p", p=P)),
                (scr[112:128, 2 * P:3 * P], t["norm2_g_2"].rearrange("l (c p) -> (l c) p", p=P)),
                (scr[0:96, 3 * P:4 * P], t["ada_b_2"].rearrange("l (c p) -> (l c) p", p=P)),
                (m_alog4, t["even_a_log"][0].partition_broadcast(P)),
                (m_dtb4, t["even_dt_bias"][0].partition_broadcast(P)),
                (m_dtb, t["odd_dt_bias"][0].partition_broadcast(P)),
                (m_alog, t["odd_a_log"][0].partition_broadcast(P)),
                (m_dskip, t["odd_d_skip"][0].partition_broadcast(P)),
                (lev[:], const[:, C_LEV:C_LEV + 7 * P].rearrange("p (c n) -> p c n", c=7)),
                (e_mask, const[:, C_ATTN:C_ATTN + 384]),
                (rope[:], const[:, C_ROPE:C_ROPE + 128].rearrange("p (k b n) -> p k b n", k=2, b=TB)),
                (iota[:], const[:, C_IOTA:C_IOTA + P + 8]),
            ] + [(m_lq[:, i, :], t[f"attn_{x}_2"][0].partition_broadcast(P)) for i, x in enumerate(("lq1", "lk1", "lq2", "lk2"))]
            for dst, src in boots:
                sp.dma_start(dst, src).then_inc(boot, 16)

            def load(s):
                src, chunks, width = slots[s]
                if s >= RING:
                    sp.wait_ge(hi_done, n.gran(2 * (s - RING + 1)))
                    sp.wait_ge(lo_done, n.gran(2 * (s - RING + 1)))
                dst = w_raw[:, s % RING, 0:chunks * width].rearrange("p (c n) -> p c n", n=width)
                sp.dma_start(dst, src).then_inc(w_landed[s % RING], 16)

            for s in range(n_slots):
                load(s)
            sp.wait_ge(mo_ids, n(mo_ids))
            n_blocks = sp.value_load(eid[0:1, 11:12], min_val=N_EXPERTS, max_val=N_EXPERTS + MAX_EXTRA)
            with sp.Fori(1, n_blocks) as b:
                e = sp.value_load(eid[0:1, bass.ds(b, 1)], min_val=0, max_val=N_EXPERTS - 1)
                n.block = b
                del slots[moe_from:]
                plan_ff(t["moe_w1_2"][0, bass.ds(e, 1)][0], t["moe_w3_2"][0, bass.ds(e, 1)][0],
                        t["moe_w2_2"][0, bass.ds(e, 1)][0], FF2)
                for s in range(moe_from, n_slots):
                    load(s)
            n.block = None
            for tb in range(TB):
                sp.wait_ge(fin, n(fin))
                sp.dma_start(out[0, tb * P:(tb + 1) * P, :], xn[:, tb, :]).then_inc(out_done, 16)
            sp.wait_ge(out_done, n(out_done, 32))

        @block.gpsimd
        def _(pool):
            n = Count()

            def modulation(l):
                def load(j):
                    nb, k = divmod(j, 4)
                    src = t["ada_w_2"][l, 2 * P * k:2 * P * (k + 1), DM * nb:DM * (nb + 1)].rearrange("(c p) n -> p c n", p=P)
                    pool.dma_start(m_w[:, j % 2], src).then_inc(ada_in[j % 2], 16)

                load(0)
                load(1)
                for j in range(24):
                    nb, k = divmod(j, 4)
                    cols = slice(DM * nb, DM * (nb + 1))
                    pool.wait_ge(ada_in[j % 2], n(ada_in[j % 2], 16))
                    for c in range(2):
                        sums = [(m_sumc, 8)] if l == 0 and nb < 2 else []
                        for dst, of in sums + [(m_sum, 0)]:
                            w, x = m_w[:, j % 2, c, :], silc[:, of + 2 * k + c:of + 2 * k + c + 1]
                            if k == 0 and c == 0:
                                pool.tensor_scalar(dst[:, cols], w, x, 0.0, ALU.mult, ALU.add).then_inc(ada_sum, 1)
                                continue
                            product = m_sum[:, 4 * DM:5 * DM] if of else w
                            pool.tensor_scalar(product, w, x, 0.0, ALU.mult, ALU.add).then_inc(ada_mul, 1)
                            pool.wait_ge(ada_mul, n(ada_mul))
                            pool.tensor_tensor(dst[:, cols], dst[:, cols], product, ALU.add).then_inc(ada_sum, 1)
                        pool.wait_ge(ada_sum, n(ada_sum, 1 + len(sums)))
                    if j + 2 < 24:
                        load(j + 2)

            def rotate(x, tb):
                def link(ins):
                    ins.then_inc(rope_link, 1)
                    pool.wait_ge(rope_link, n(rope_link))
                v = x.rearrange("p (g a s f) -> p g a s f", g=16, a=2, s=2)
                x1, x2 = v[:, :, :, 0, :], v[:, :, :, 1, :]
                cs, sn = [rope[:, k, tb, :].rearrange("p (a f) -> p a f", a=2).unsqueeze(1).to_broadcast([P, 16, 2, 16])
                          for k in range(2)]
                t1, t2 = [wbc[:, 512 * k:512 * k + 512].rearrange("p (g a f) -> p g a f", g=16, a=2) for k in range(2)]
                pool.tensor_tensor(t1, x1, sn, ALU.mult)
                link(pool.tensor_tensor(t2, x2, sn, ALU.mult))
                pool.tensor_tensor(x1, x1, cs, ALU.mult)
                link(pool.tensor_tensor(x2, x2, cs, ALU.mult))
                pool.tensor_tensor(x1, x1, t2, ALU.subtract)
                link(pool.tensor_tensor(x2, x2, t1, ALU.add))

            pool.wait_ge(h_ready, n(h_ready, 2))
            modulation(0)
            pool.wait_ge(h_ready, n(h_ready, 3))
            pool.dma_start(ctx_x, t["ctx_2"][0].rearrange("(b p) n -> p b n", p=P)).then_inc(ctx_in, 16)
            for i, (x, at) in enumerate(((xn, 0), (da_k, 2))):
                pool.wait_ge(proj_out, 19 + 2 * (i + 1))
                rotate(x[:, at, :], 0)
                rotate(x[:, at + 1, :], 1)
                pool.tensor_copy(r_ids[:, 0:1], ones[:, 0:1]).then_inc(rope_done, 1)
            pool.wait_ge(h_ready, n(h_ready, 2))
            pool.dma_start(f_g, const[:, C_DFTG:C_DFTG + 256]).then_inc(tab_in, 16)
            pool.dma_start(f_l, const[:, C_DFTL:C_DFTL + 1024].rearrange("p (k b n) -> p k b n", k=2, b=TB)).then_inc(tab_in, 16)
            for k in range(2):
                c = slice(4 * k, 4 * k + 4)
                pool.dma_start(r_w[:, c, :], t["moe_router_2"][0].rearrange("(c p) e -> p c e", p=P)[:, c, :]).then_inc(tab_in, 16)
            modulation(1)

        SPREAD_AT, ADDED_AT, GATES_AT, PLACES_AT, GATHER_AT, GATHERED_AT = 0, 1, 2, 3, 4, 5
        mo_xe = [xt[:, 512:1024], xt[:, 1536:2048]]

        FF_STEPS = len(steps(FF2))
        PER_BLOCK = {x.name: FF_STEPS for x in (silu_done, hid_done, hid_t, hid_x, hhi_done, hlo_done)}
        PER_BLOCK |= {x.name: 1 for x in (mo_p, mo_pt, mo_ptc, mo_y, mo_c, mo_cc)}
        PER_BLOCK |= {x.name: 2 for x in (mo_x, mo_xc, mo_xh, mo_xl)}
        PER_BLOCK |= {mo_link.name: 1}

        def start_blocks(n, b):
            n.block, n.per, n.before = b, PER_BLOCK, dict(n.at)

        def end_blocks(n):
            for name, k in n.at.items():
                assert k - n.before.get(name, 0) in (0, PER_BLOCK.get(name, 0)), name
            n.block = None

        BOOT = 16 * 29

        def granule(s, j):
            _, chunks, width = slots[s]
            return chunks // 2, width, j * (chunks // 2) * width

        @block.scalar
        def _(act):
            n = Count()
            at = [0]
            ahead = [0]

            def split(k):
                for s in range(at[0] + ahead[0], at[0] + k):
                    act.wait_ge(w_landed[s % RING], n.ring(16 * (s // RING + 1)))
                    for j in range(2):
                        g = 2 * s + j
                        c, width, o = granule(s, j)
                        if g >= SPLITS:
                            act.wait_ge(gran_used, n.gran(g - SPLITS + 1))
                        act.activation(w_hi[:, g % SPLITS, 0:c * width], w_raw[:, s % RING, o:o + c * width],
                                       ACT.Copy).then_inc(hi_done, 1)
                at[0] += k
                ahead[0] = 0

            def split_ahead(k=2):
                split(k)
                at[0] -= k
                ahead[0] = k

            def sqrt_stats(k):
                act.wait_ge(ms_done, n(ms_done))
                act.activation(rt[:, 0:k], ms[:, 0:k], ACT.Sqrt).then_inc(rt_done, 1)

            def sum_squares(src, of_h=False):
                for tb in range(TB):
                    if of_h:
                        landed = h_ready if tb else h_first
                        act.wait_ge(landed, n(landed))
                    act.activation(xn[:, tb, :], src(tb), ACT.Square, accum_out=ssq[:, tb:tb + 1]).then_inc(sq_done, 1)
                sqrt_stats(TB)

            def split_act(rounds=1, base=0):
                for r in range(rounds):
                    for b in range(4):
                        act.wait_ge(xt_done, n(xt_done))
                        c = base + 8 * r + 2 * b
                        act.activation(act_hi[:, c:c + 2, :], xt[:, 512 * b:512 * b + 512].rearrange("p (c n) -> p c n", c=2),
                                       ACT.Copy).then_inc(ahi_done, 1)

            def norm(first=False, src=h, base=0):
                if first:
                    act.wait_ge(boot, BOOT)
                elif src is not h:
                    act.wait_ge(ctx_in, 16)
                sum_squares(lambda tb: src[:, tb, :], of_h=src is h and not first)
                split_act(base=base)

            def gated(ff, tbs=TB, beside=None):
                s = steps(ff)

                def hidden(i):
                    c = s[i][1] // P
                    act.wait_ge(hid_x, n(hid_x))
                    src = xt[:, 1024 * (i % 2):1024 * (i % 2) + c * tbs * P].rearrange("p (c n) -> p c n", c=c)
                    base = 8 + 4 * (i % 2)
                    act.activation(act_hi[:, base:base + c, 0:tbs * P], src, ACT.Copy).then_inc(hhi_done, 1)

                for i, (_, width) in enumerate(s):
                    per = 2 if width == BANK else 1
                    split(per)
                    if beside:
                        beside(i)
                    if i:
                        hidden(i - 1)
                    split(per)
                    act.wait_ge(gran_used, n.gran(2 * (at[0] - per)))
                    if i:
                        act.wait_ge(hid_done, n(hid_done))
                    act.activation(sg[:, 0:tbs * BANK].rearrange("p (b n) -> p b n", b=tbs)[:, :, 0:width],
                                   ps[:, 4:4 + tbs, 0:width], ACT.Silu).then_inc(silu_done, 1)
                    if i:
                        split(2 if s[i - 1][1] == BANK else 1)
                n(hid_done)
                hidden(len(s) - 1)
                split(2 if s[-1][1] == BANK else 1)
                if beside:
                    beside(len(s))

            def residual():
                act.wait_ge(gran_used, 2 * at[0])
                sum_squares(lambda tb: banks(2 * tb, 2))
                if at[0] + 2 <= n_slots:
                    split_ahead()

            def even():
                for j in range(8):
                    split(2 if j < 7 else 1)
                    if j:
                        even_out(j - 1)
                even_out(7)

                def exps(i):
                    act.wait_ge(at_mx, n(at_mx))
                    for tb, k in ((0, slice(0, P)), (1, slice(P, 3 * P))):
                        ins = act.activation(a_p[:, i % 2, k], a_s[:, i % 2, k], ACT.Exp,
                                             bias=w8(30 + i % 2, 2)[:, tb:tb + 1], accum_out=w8(32 + i % 2, 2)[:, tb:tb + 1])
                    ins.then_inc(at_p, 1)

                for f in range(6):
                    act.wait_ge(cv_done, n(cv_done))
                    c = e_cv[:, 2 * f:2 * f + 2, :]
                    act.activation(c, c, ACT.Silu).then_inc(cv_act, 1)
                for i in range(A_HEADS):
                    exps(i)

                act.wait_ge(sv_in, n(sv_in))
                act.activation(w8(8), w8(7), ACT.Exp, scale=-1.0).then_inc(act_link, 1)
                act.wait_ge(act_link, n(act_link))
                act.activation(w8(9), w8(8), ACT.Ln, bias=1.0)
                act.activation(w8(10).rearrange("p (b n) -> p b n", b=TB), e_ba[:, :, 0:4], ACT.Exp, scale=-1.0)
                act.activation(w8(11, 4), m_alog4, ACT.Exp).then_inc(sv_out, 1)
                act.wait_ge(sv_in, n(sv_in))
                act.activation(w8(4), w8(2), ACT.Exp)
                act.activation(w8(5), w8(12), ACT.Exp).then_inc(sv_out, 1)

                for T in range(TB):
                    sqrt_stats(8)
                    act.wait_ge(dl_R, n(dl_R))
                    for i in range(B_HEADS):
                        ins = act.activation(d_DT[:, i, :], ps[:, 7, i * P:(i + 1) * P], ACT.Exp,
                                             bias=w8(6)[:, 4 * T + i:4 * T + i + 1])
                    ins.then_inc(dl_dt, 1)
                    for i, dst in enumerate((d_qT, d_kT, d_kbT, d_qdT)):
                        act.wait_ge(dl_t3, n(dl_t3))
                        act.activation(dst, ps[:, 3 + i, :].rearrange("p (c n) -> p c n", c=4), ACT.Copy).then_inc(dl_tc, 1)
                    for level in range(1, 7):
                        act.wait_ge(dl_y, n(dl_y))
                        act.activation(d_Y, ps[:, 3, :].rearrange("p (c n) -> p c n", c=4), ACT.Copy).then_inc(dl_yc, 1)
                    sqrt_stats(4)
                split_act()
                split(4)

            def even_out(j):
                act.wait_ge(gran_used, 2 * (at[0] - (0 if j == 7 else 1 if j == 6 else 2)))
                src = ps[:, 2 * (j % 4):2 * (j % 4) + 2, :]
                if j < 3:
                    act.activation(e_qkv[:, j], src, ACT.Copy).then_inc(proj_out, 1)
                elif j < 6:
                    act.activation(e_raw[:, :, (j - 3) * BANK:(j - 2) * BANK], src, ACT.Copy).then_inc(proj_out, 1)
                elif j == 6:
                    act.activation(e_sz, src, ACT.Silu).then_inc(proj_out, 1)
                else:
                    act.activation(e_ba, src[:, :, 0:8], ACT.Copy).then_inc(proj_out, 1)

            def odd():
                def out_of_banks(j):
                    act.wait_ge(gran_used, 4 * j + 4 + base if j < 10 else 4 * 10 + 2 + base)
                    src = ps[:, 2 * (j % 2):2 * (j % 2) + 2, :]
                    if j < 4:
                        ins = act.activation(o_z[:, :, j * BANK:(j + 1) * BANK], src, ACT.Silu)
                    elif j < 10:
                        ins = act.activation(xn[:, j % 2, :].rearrange("p (b n) -> p b n", b=TB), src, ACT.Copy)
                    else:
                        ins = act.activation(dtw[:, T_X, :].rearrange("p (b n) -> p b n", b=TB), src[:, :, 0:32], ACT.Copy)
                    ins.then_inc(proj_out, 1)

                base = 2 * at[0]
                for j in range(14):
                    if j < 11:
                        split(2 if j < 10 else 1)
                    if 0 <= j - 1 < 11:
                        out_of_banks(j - 1)
                    if 4 <= j - 2 < 10:
                        for f in range(2):
                            act.wait_ge(cv_done, n(cv_done))
                            src = xt[:, 1024 * (j % 2) + 512 * f:1024 * (j % 2) + 512 * f + 512].rearrange("p (c n) -> p c n", c=2)
                            c = 4 * (j - 2 - 8) + 2 * f
                            act.activation(src if j - 2 < 8 else o_bc[:, c:c + 2, :], src, ACT.Silu).then_inc(cv_act, 1)
                    if 4 <= j - 4 < 9:
                        act.wait_ge(o_tp, n(o_tp))
                        k = j - 8
                        if k < 4:
                            ins = act.activation(o_x[:, :, k * BANK:(k + 1) * BANK], ps[:, 6:8, :], ACT.Copy)
                        else:
                            ins = act.activation(o_bt, ps[:, 6, :].rearrange("p (c n) -> p c n", c=4), ACT.Copy)
                        ins.then_inc(o_tc, 1)

                act.wait_ge(sv_in, n(sv_in))
                act.activation(dtw[:, T_E, :], dtw[:, T_ABS, :], ACT.Exp, scale=-1.0).then_inc(act_link, 1)
                act.wait_ge(act_link, n(act_link))
                act.activation(dtw[:, T_LN, :], dtw[:, T_E, :], ACT.Ln, bias=1.0)
                act.activation(work[:, 0:32], m_alog, ACT.Exp).then_inc(sv_out, 1)
                act.wait_ge(sv_in, n(sv_in))
                act.activation(dtw[:, T_ECUM, :], dtw[:, T_CUM, :], ACT.Exp)
                act.activation(dtw[:, T_EDEC, :], dtw[:, T_REST, :], ACT.Exp).then_inc(sv_out, 1)

                for g in range(C_GROUPS):
                    act.wait_ge(og_cb, n(og_cb))
                    act.activation(xt[:, 256 * (g % 2):256 * (g % 2) + 256], ps[:, 0, 0:256], ACT.Copy).then_inc(og_cc, 1)
                    for q in range(4):
                        T, m = q // 2, q % 2
                        act.wait_ge(og_R, n(og_R))
                        for i in range(4):
                            head = 32 * T + 8 * g + 4 * m + i
                            ins = act.activation(hp[:, 512 * m + i * P:512 * m + (i + 1) * P], ps[:, 2 + m, i * P:(i + 1) * P],
                                                 ACT.Exp, bias=dtw[:, T_NCUM, head:head + 1])
                        ins.then_inc(og_e, 1)
                        if q == 0:
                            act.wait_ge(og_s, n(og_s))
                            act.activation(o_st, ps[:, 6, :], ACT.Copy).then_inc(og_sc, 1)
                    for T in range(TB):
                        act.wait_ge(og_yz, n(og_yz))
                        ins = act.activation(xn[:, T, 0:BANK], o_z[:, T, g * BANK:(g + 1) * BANK], ACT.Square,
                                             accum_out=ssq[:, 4 * T + g:4 * T + g + 1])
                        ins.then_inc(act_link, 1)
                        act.wait_ge(act_link, n(act_link))
                act.activation(xn[:, 0, 0:1], ones[:, 0:1], ACT.Copy).then_inc(sq_done, 1)
                sqrt_stats(8)
                split_act(rounds=2)
                split(8)

            def diff_attention():
                base = 2 * at[0]
                for j in range(7):
                    if j < 6:
                        split(2)
                    if j:
                        k, b = j - 1, 4 * ((j - 1) % 2)
                        act.wait_ge(gran_used, base + 4 * j)
                        cols = slice((k % 2) * BANK, (k % 2 + 1) * BANK)
                        dst, tbs = ((xn[:, :, cols], TB), (da_k[:, :, cols], 4), (da_v[:, :, cols], 4))[k // 2]
                        act.activation(dst, ps[:, b:b + tbs, :], ACT.Copy).then_inc(proj_out, 1)
                for b in range(4):
                    act.wait_ge(da_qt, n(da_qt))
                    dst = (sg if b < 2 else hp)[:, (b % 2) * BANK:(b % 2 + 1) * BANK]
                    act.activation(dst, ps[:, b, :], ACT.Copy).then_inc(da_qc, 1)
                act.wait_ge(sv_in, n(sv_in))
                act.activation(w8(43, 2), w8(44, 2), ACT.Exp).then_inc(sv_out, 1)

                def exps(u):
                    act.wait_ge(da_m, n(da_m))
                    if u >= 2:
                        act.wait_ge(da_a, u - 1)
                    for k in range(2):
                        ins = act.activation(xt[:, 1024 * (u % 2) + 512 * k:1024 * (u % 2) + 512 * k + 512],
                                             ps[:, 2 * (u % 2) + k, :], ACT.Exp, scale=DA_DIM ** -0.5,
                                             bias=w8(40)[:, 2 * (u % 2) + k:2 * (u % 2) + k + 1],
                                             accum_out=w8(41)[:, 2 * (u % 2) + k:2 * (u % 2) + k + 1])
                    ins.then_inc(da_e, 1)

                units = TB * DA_HEADS
                exps(0)
                exps(1)
                for u in range(units):
                    act.wait_ge(da_at, n(da_at))
                    if u >= 2:
                        act.wait_ge(da_o, u - 1)
                    act.activation(da_aT[:, u % 2, :], ps[:, 4 + u % 2, :], ACT.Copy).then_inc(da_ac, 1)
                    if u + 2 < units:
                        exps(u + 2)
                    act.wait_ge(da_o, n(da_o))
                    head, tb = u // 2, u % 2
                    o = ps[:, 6 + u % 2, 0:P]
                    act.activation(xn[:, tb, head * P:(head + 1) * P], o, ACT.Copy)
                    act.activation(da_sq[:, u, :], o, ACT.Square, accum_out=ssq[:, 8 * tb + head:8 * tb + head + 1]).then_inc(da_oc, 1)
                sqrt_stats(16)
                split_act()
                split(4)

            def fourier():
                sum_squares(lambda tb: h[:, tb, :], of_h=True)
                for g in range(8):
                    act.wait_ge(ft_x, n(ft_x))
                    act.activation(f_z(g), ps[:, g, :].rearrange("p (b n) -> p b n", b=TB), ACT.Copy).then_inc(ft_c, 1)
                n(xt_done, 4)
                split_act()
                split(4)

            def experts():
                def gathered():
                    for k in range(2):
                        act.wait_ge(mo_xc, n(mo_xc))
                        act.activation(act_hi[:, 4 * k:4 * k + 4, 0:P], mo_xe[k].rearrange("p (c n) -> p c n", c=4),
                                       ACT.Copy).then_inc(mo_xh, 1)

                sum_squares(lambda tb: h[:, tb, :], of_h=True)
                act.wait_ge(mo_v, n(mo_v))
                act.activation(r_e, r_d, ACT.Exp).then_inc(mo_ex, 1)
                gathered()
                act.wait_ge(mo_ids, n(mo_ids))
                n_blocks = act.value_load(eid[0:1, 11:12], min_val=N_EXPERTS, max_val=N_EXPERTS + MAX_EXTRA)
                with act.Fori(0, n_blocks) as b:
                    start_blocks(n, b)
                    before = 2 * at[0]

                    def beside(i):
                        if i == SPREAD_AT:
                            act.wait_ge(gran_used, n.gran(before))
                            act.activation(mo_ye, banks(0, 2), ACT.Copy).then_inc(mo_y, 1)
                        if i == GATES_AT + 1:
                            act.wait_ge(mo_pt, n(mo_pt))
                            act.activation(mo_PT, ps[:, 3, 0:TOKENS].rearrange("p (b n) -> p b n", b=TB), ACT.Copy).then_inc(mo_ptc, 1)
                        if i == FF_STEPS:
                            act.wait_ge(gran_used, n.gran(2 * (at[0] - 4)))
                            gathered()
                    gated(FF2, 1, beside)
                    end_blocks(n)
                act.wait_ge(mo_end, n(mo_end))
                act.activation(mo_ye, banks(0, 2), ACT.Copy).then_inc(mo_end_y, 1)
                act.wait_ge(h_ready, n(h_ready))
                sum_squares(lambda tb: h[:, tb, :])

            norm(first=True)
            act.activation(silc, colv[:, V_C:V_C + 16], ACT.Silu)
            gated(FF1)
            residual()
            norm()
            even()
            residual()
            norm()
            gated(FF1)
            residual()
            norm()
            gated(FF1)
            residual()
            norm()
            odd()
            residual()
            norm()
            gated(FF1)
            residual()

            norm()
            norm(src=ctx_x, base=8)
            diff_attention()
            if at[0] + 2 <= n_slots:
                split_ahead()
            norm()
            gated(FF2)
            if at[0] + 2 <= n_slots:
                split_ahead()
            fourier()
            experts()

        @block.vector
        def _(dve):
            n = Count()
            at = [0]
            ahead = [0]

            def link(ins):
                ins.then_inc(dve_link, 1)
                dve.wait_ge(dve_link, n(dve_link))

            def split(k):
                for s in range(at[0] + ahead[0], at[0] + k):
                    for j in range(2):
                        g = 2 * s + j
                        c, width, o = granule(s, j)
                        dve.wait_ge(hi_done, n.gran(g + 1))
                        dve.tensor_tensor(w_lo[:, g % SPLITS, 0:c * width], w_raw[:, s % RING, o:o + c * width],
                                          w_hi[:, g % SPLITS, 0:c * width].bitcast(F32), ALU.subtract).then_inc(lo_done, 1)
                at[0] += k
                ahead[0] = 0

            def split_ahead(k=2):
                split(k)
                at[0] -= k
                ahead[0] = k

            def inverse_rms(k, scale):
                dve.tensor_scalar(ms[:, 0:k], ssq[:, 0:k], scale, EPS, ALU.mult, ALU.add).then_inc(ms_done, 1)
                dve.wait_ge(rt_done, n(rt_done))
                link(dve.reciprocal(rstd[:, 0:k], rt[:, 0:k]))

            def split_act(rounds=1, base=0, scale=None, bias=None):
                for r in range(rounds):
                    for b in range(6):
                        if b < 4:
                            dve.wait_ge(tp_done, n(tp_done))
                            for c in (2 * b, 2 * b + 1):
                                src, dst = ps[:, b, (c % 2) * TOKENS:(c % 2 + 1) * TOKENS], xt[:, c * TOKENS:(c + 1) * TOKENS]
                                if scale is None:
                                    ins = dve.tensor_copy(dst, src)
                                elif bias is None:
                                    ins = dve.tensor_scalar(dst, src, scale(8 * r + c), None, ALU.mult)
                                else:
                                    ins = dve.tensor_scalar(dst, src, scale(8 * r + c), bias(8 * r + c), ALU.mult, ALU.add)
                            ins.then_inc(xt_done, 1)
                        if b >= 2:
                            dve.wait_ge(ahi_done, n(ahi_done))
                            c = base + 8 * r + 2 * (b - 2)
                            dve.tensor_tensor(act_lo[:, c:c + 2, :], xt[:, 512 * (b - 2):512 * (b - 1)].rearrange("p (c n) -> p c n", c=2),
                                              act_hi[:, c:c + 2, :].bitcast(F32), ALU.subtract).then_inc(alo_done, 1)
                    dve.wait_ge(alo_done, n(alo_done, 4))

            def norm(scale, bias=None, src=h, base=0):
                dve.wait_ge(sq_done, n(sq_done, TB))
                inverse_rms(TB, 1.0 / DM)
                for tb in range(TB):
                    dve.tensor_scalar(xn[:, tb, :], src[:, tb, :], rstd[:, tb:tb + 1], None, ALU.mult).then_inc(xn_done, 1)
                split_act(base=base, scale=scale, bias=bias)

            def gated(ff, tbs=TB, beside=None):
                s = steps(ff)

                def hidden(i):
                    c = s[i][1] // P
                    dve.wait_ge(hid_t, n(hid_t))
                    x = xt[:, 1024 * (i % 2):1024 * (i % 2) + c * tbs * P]
                    dve.tensor_copy(x, banks(6, tbs)[:, 0:c * tbs * P]).then_inc(hid_x, 1)
                    dve.wait_ge(hhi_done, n(hhi_done))
                    base = 8 + 4 * (i % 2)
                    dve.tensor_tensor(act_lo[:, base:base + c, 0:tbs * P], x.rearrange("p (c n) -> p c n", c=c),
                                      act_hi[:, base:base + c, 0:tbs * P].bitcast(F32), ALU.subtract).then_inc(hlo_done, 1)

                for i, (_, width) in enumerate(s):
                    per = 2 if width == BANK else 1
                    split(per)
                    if i:
                        hidden(i - 1)
                    if beside and i in (ADDED_AT, GATHERED_AT):
                        beside(i)
                    split(per)
                    up_end = at[0]
                    if i:
                        split(2 if s[i - 1][1] == BANK else 1)
                    dve.wait_ge(silu_done, n(silu_done))
                    dve.wait_ge(gran_used, n.gran(2 * up_end))
                    view = [x[:, 0:tbs * BANK].rearrange("p (b n) -> p b n", b=tbs)[:, :, 0:width] for x in (hp, sg)]
                    dve.tensor_tensor(view[0], view[1], ps[:, 6:6 + tbs, 0:width], ALU.mult).then_inc(hid_done, 1)
                    if beside and i == PLACES_AT:
                        beside(i)
                hidden(len(s) - 1)
                split(2 if s[-1][1] == BANK else 1)
                if beside:
                    beside(len(s))

            def row_diag(col):
                dve.tensor_tensor(sg[:].rearrange("p (c n) -> p c n", c=DC), bc_mid(ident, DC), bc(col, P),
                                  ALU.mult).then_inc(diag_done, 1)

            def row_copy():
                dve.wait_ge(bc_ready, n(bc_ready))
                link(dve.tensor_copy(wbc[:], banks(6, 2)))

            def residual(col, factor):
                row_diag(col)
                row_copy()
                dve.wait_ge(sq_done, n(sq_done, TB))
                inverse_rms(TB, 1.0 / DM)
                for tb in range(TB):
                    link(dve.scalar_tensor_tensor(xn[:, tb, :], banks(2 * tb, 2), rstd[:, tb:tb + 1], wbc[:], ALU.mult, ALU.mult))
                    dve.scalar_tensor_tensor(h[:, tb, :], xn[:, tb, :], factor, h[:, tb, :],
                                             ALU.mult, ALU.add).then_inc(h_ready if tb else h_first, 1)
                if at[0] + 2 <= n_slots:
                    split_ahead(1)

            def nw(l, j):
                return colv[:, V_NW + 48 * l + 8 * j:V_NW + 48 * l + 8 * j + 8]

            def scaled(dst, src, col):
                return dve.tensor_tensor(dst, src, bc(col, P), ALU.mult)

            def softplus_in(dst_x, dst_abs, x, bias):
                link(dve.tensor_tensor(dst_x, x, bias, ALU.add))
                link(dve.tensor_scalar(dst_abs, dst_x, -1.0, None, ALU.mult))
                dve.tensor_tensor(dst_abs, dst_abs, dst_x, ALU.max).then_inc(sv_in, 1)

            def even():
                split(15)
                for i, dst in enumerate((e_qt, e_qt, e_kt, e_kt)):
                    dve.wait_ge(qk_tp, n(qk_tp))
                    dve.tensor_copy(dst[:, 2 * (i % 2):2 * (i % 2) + 2, :],
                                    ps[:, 4 + i, :].rearrange("p (c n) -> p c n", c=2)).then_inc(qk_cp, 1)

                def masked(i):
                    dve.wait_ge(at_sc, n(at_sc))
                    m = w8(30 + i % 2, 2)
                    link(dve.scalar_tensor_tensor(a_s[:, i % 2, :], ps[:, 4 + i % 2, 0:384], A_DIM ** -0.5, e_mask, ALU.mult, ALU.add))
                    dve.tensor_reduce(m[:, 0:1], a_s[:, i % 2, 0:P], AX_X, ALU.max)
                    link(dve.tensor_reduce(m[:, 1:2], a_s[:, i % 2, P:384], AX_X, ALU.max))
                    dve.tensor_scalar(m, m, -1.0, None, ALU.mult).then_inc(at_mx, 1)

                def convolve(f):
                    dve.wait_ge(cv_tp, n(cv_tp))
                    for k in range(CONV_K):
                        for c in (2 * f, 2 * f + 1):
                            w = colv[:, V_ECONV + (3 - k) * 12 + c:V_ECONV + (3 - k) * 12 + c + 1]
                            src = ps[:, f % 2, (c % 2) * TOKENS:(c % 2 + 1) * TOKENS]
                            if k == 0:
                                ins = dve.tensor_scalar(e_cv[:, c, :], src, w, None, ALU.mult)
                            else:
                                ins = dve.scalar_tensor_tensor(e_cv[:, c, k:], src[:, 0:TOKENS - k], w, e_cv[:, c, k:], ALU.mult, ALU.add)
                        if k < CONV_K - 1:
                            link(ins)
                    ins.then_inc(cv_done, 1)

                for f in range(6):
                    convolve(f)
                masked(0)
                for i in range(A_HEADS):
                    if i + 1 < A_HEADS:
                        masked(i + 1)
                    dve.wait_ge(at_pt, n(at_pt))
                    dve.tensor_copy(a_pt[:, i % 2, :], ps[:, 6 + i % 2, 0:384]).then_inc(at_pc, 1)
                    link(dve.reciprocal(w8(34 + i % 2, 2), w8(32 + i % 2, 2)))
                    dve.wait_ge(at_pv, n(at_pv))
                    for tb in range(TB):
                        ins = dve.tensor_scalar(xn[:, tb, i * A_DIM:(i + 1) * A_DIM], ps[:, 2 + i % 2, tb * A_DIM:(tb + 1) * A_DIM],
                                                w8(34 + i % 2, 2)[:, tb:tb + 1], None, ALU.mult)
                    ins.then_inc(at_o, 1)

                def two(ap):
                    return ap.rearrange("p (b n) -> p b n", b=TB)

                softplus_in(two(w8(1)), two(w8(7)), e_ba[:, :, 4:8], bc_mid(m_dtb4, TB))
                dve.wait_ge(sv_out, n(sv_out))
                link(dve.scalar_tensor_tensor(w8(1), w8(1), 0.0, w8(9), ALU.max, ALU.add))
                link(dve.scalar_tensor_tensor(two(w8(1)), two(w8(1)), -1.0, bc_mid(w8(11, 4), TB), ALU.mult, ALU.mult))
                link(dve.tensor_scalar(w8(0), w8(10), 1.0, None, ALU.add))
                dve.reciprocal(w8(0), w8(0))
                dve.tensor_scalar(sg[:, 0:P], ident, colv[:, V_HNW:V_HNW + 1], None, ALU.mult).then_inc(dl_g, 1)
                dve.wait_ge(dl_gc, n(dl_gc))
                link(dve.tensor_copy(work[:, 16:32], ps[:, 0, 0:16]))
                dve.tensor_tensor(w8(12), w8(3), w8(2), ALU.subtract)
                dve.tensor_scalar(w8(6), w8(2), -1.0, None, ALU.mult)
                dve.tensor_copy(wbc[:, 0:P], ps[:, 1, 0:P]).then_inc(sv_in, 1)
                dve.wait_ge(sv_out, n(sv_out))

                for T in range(TB):
                    def col(i):
                        return w8(i)[:, 4 * T:4 * T + 4]
                    for b in range(3):
                        dve.wait_ge(dl_tm, n(dl_tm))
                        ins = dve.tensor_copy(d_tm[:, 4 * b:4 * b + 4, :], ps[:, b, :].rearrange("p (c n) -> p c n", c=4))
                    link(ins)
                    sq = hp[:].rearrange("p (c n) -> p c n", c=8)
                    link(dve.tensor_tensor(sq, d_tm[:, 0:8, :], d_tm[:, 0:8, :], ALU.mult))
                    link(dve.tensor_reduce(ssq[:, 0:8], sq, AX_X, ALU.add))
                    inverse_rms(8, 1.0)
                    link(dve.tensor_scalar(rstd[:, 0:4], rstd[:, 0:4], B_DIM ** -0.5, None, ALU.mult))
                    link(scaled(d_tm[:, 0:8, :], d_tm[:, 0:8, :], rstd[:, 0:8]))
                    scaled(d_qd, d_tm[:, 0:4, :], col(4))
                    scaled(d_kb, d_tm[:, 4:8, :], col(0)).then_inc(dl_in, 1)
                    dve.tensor_tensor(d_A, bc_mid(tri, 4), bc(col(1), P), ALU.mult).then_inc(dl_lg, 1)
                    scaled(d_tm[:, 8:12, :], d_tm[:, 8:12, :], col(0))
                    dve.wait_ge(dl_in, n(dl_in))
                    scaled(d_kbg, d_kb, col(4))
                    scaled(d_kd, d_tm[:, 4:8, :], col(5))

                    def heads(b):
                        return ps[:, b, :].rearrange("p (c n) -> p c n", c=4)

                    def off(level):
                        dve.tensor_tensor(d_off[level % 2], d_A, bc_mid(lev[:, level, :], 4), ALU.mult).then_inc(dl_off, 1)

                    dve.wait_ge(dl_dt, n(dl_dt))
                    dve.wait_ge(dl_at, n(dl_at))
                    link(dve.tensor_tensor(d_A, heads(0), d_DT, ALU.mult))
                    dve.tensor_tensor(d_QK, heads(1), d_DT, ALU.mult)
                    link(dve.tensor_tensor(d_Y, d_A, bc_mid(lev[:, 0, :], 4), ALU.mult))
                    dve.tensor_tensor(d_XT, bc_mid(ident, 4), d_Y, ALU.subtract).then_inc(dl_xt, 1)
                    off(1)
                    dve.wait_ge(dl_xtt, n(dl_xtt))
                    dve.tensor_copy(d_X, heads(2)).then_inc(dl_x, 1)
                    for level in range(1, 7):
                        if level < 6:
                            off(level + 1)
                        dve.wait_ge(dl_xy, n(dl_xy))
                        ins = dve.tensor_tensor(d_XT, d_XT, heads(4), ALU.subtract)
                        if level < 6:
                            ins = dve.tensor_tensor(d_X, d_X, heads(5), ALU.subtract)
                        ins.then_inc(dl_x, 1)
                    dve.wait_ge(dl_u, n(dl_u))
                    if T == 0:
                        dve.tensor_copy(d_kbT, heads(6)).then_inc(dl_vn, 1)
                    else:
                        dve.tensor_copy(d_DT, heads(6))
                        dve.tensor_copy(d_kT, heads(7)).then_inc(dl_uc, 1)
                        dve.wait_ge(dl_ws, n(dl_ws))
                        dve.tensor_tensor(d_kbT, d_DT, heads(2), ALU.subtract).then_inc(dl_vn, 1)
                    dve.wait_ge(dl_o, n(dl_o))
                    if T == 0:
                        dve.tensor_copy(d_S, heads(1))
                    link(dve.tensor_copy(d_qT, heads(0)))
                    link(dve.tensor_tensor(d_Y, d_qT, d_qT, ALU.mult))
                    link(dve.tensor_reduce(ssq[:, 0:4], d_Y, AX_X, ALU.add))
                    inverse_rms(4, 1.0 / B_DIM)
                    link(scaled(d_qT, d_qT, rstd[:, 0:4]))
                    link(dve.tensor_tensor(d_qT, d_qT, bc_mid(wbc[:, 0:P], 4), ALU.mult))
                    dve.tensor_tensor(xn[:, T, BANK:DM], d_qT.rearrange("p c n -> p (c n)"), e_sz[:, T, :], ALU.mult).then_inc(xn_done, 1)
                split_act()
                split(4)

            def odd():
                for j in range(12):
                    if j < 11:
                        split(2 if j < 10 else 1)
                    if 4 <= j - 2 < 10:
                        if j - 4 >= 4:
                            dve.wait_ge(o_tp, n(o_tp))
                        for f in range(2):
                            dve.wait_ge(cv_tp, n(cv_tp))
                            for k in range(CONV_K):
                                for c in range(2):
                                    v = 4 * (j - 6) + 2 * f + c
                                    w = colv[:, V_OCONV + (3 - k) * 24 + v:V_OCONV + (3 - k) * 24 + v + 1]
                                    dst = xt[:, 1024 * (j % 2) + 512 * f + TOKENS * c:1024 * (j % 2) + 512 * f + TOKENS * (c + 1)]
                                    src = ps[:, 4 + f, c * TOKENS:(c + 1) * TOKENS]
                                    if k == 0:
                                        ins = dve.tensor_scalar(dst, src, w, colv[:, V_OCB + v:V_OCB + v + 1], ALU.mult, ALU.add)
                                    else:
                                        ins = dve.scalar_tensor_tensor(dst[:, k:], src[:, 0:TOKENS - k], w, dst[:, k:], ALU.mult, ALU.add)
                                if k < CONV_K - 1:
                                    link(ins)
                            ins.then_inc(cv_done, 1)
                n(o_tp)

                def two(k):
                    return dtw[:, k, :].rearrange("p (b n) -> p b n", b=TB)

                dve.wait_ge(proj_out, 8 + 11)
                softplus_in(two(T_X), two(T_ABS), two(T_X), bc_mid(m_dtb, TB))
                dve.wait_ge(sv_out, n(sv_out))
                link(dve.scalar_tensor_tensor(dtw[:, T_DT, :], dtw[:, T_X, :], 0.0, dtw[:, T_LN, :], ALU.max, ALU.add))
                dve.scalar_tensor_tensor(two(T_A), two(T_DT), -1.0, bc_mid(work[:, 0:32], TB), ALU.mult, ALU.mult).then_inc(dl_g, 1)
                dve.wait_ge(dl_gc, n(dl_gc))
                link(dve.tensor_copy(dtw[:, T_CUM:T_TOT + 1, :], ps[:, 0, 0:128].rearrange("p (k n) -> p k n", k=2)))
                dve.tensor_tensor(dtw[:, T_REST, :], dtw[:, T_TOT, :], dtw[:, T_CUM, :], ALU.subtract)
                dve.tensor_scalar(dtw[:, T_NCUM, :], dtw[:, T_CUM, :], -1.0, None, ALU.mult).then_inc(sv_in, 1)
                dve.wait_ge(sv_out, n(sv_out))

                def of(k, T, g, m=0, heads=C_REP):
                    return dtw[:, k, 32 * T + 8 * g + 4 * m:32 * T + 8 * g + 4 * m + heads]

                def eight(ap):
                    return ap.rearrange("p (c n) -> p c n", c=C_REP)

                def masked_decays(g, q):
                    T, m = q // 2, q % 2
                    dst = sg[:, 512 * m:512 * m + 512].rearrange("p (c n) -> p c n", c=4)
                    dve.tensor_tensor(dst, bc_mid(tri, 4), bc(of(T_A, T, g, m, 4), P), ALU.mult).then_inc(og_la, 1)

                masked_decays(0, 0)
                for g in range(C_GROUPS):
                    cols = slice(g * BANK, (g + 1) * BANK)
                    if g == 0:
                        dve.wait_ge(o_tc, 5)
                    dve.tensor_tensor(eight(o_xdt[:, 1, :]), eight(o_x[:, 1, cols]), bc(of(T_DT, 1, g), C_DIM), ALU.mult)
                    link(dve.tensor_tensor(eight(o_xdt[:, 0, :]), eight(o_x[:, 0, cols]), bc(of(T_DT, 0, g), C_DIM), ALU.mult))
                    dve.tensor_tensor(eight(o_xd), eight(o_xdt[:, 0, :]), bc(of(T_EDEC, 0, g), C_DIM), ALU.mult).then_inc(og_x, 1)
                    dve.wait_ge(og_cc, n(og_cc))
                    for q in range(4):
                        T, m = q // 2, q % 2
                        if q < 3:
                            masked_decays(g, q + 1)
                        elif g < 3:
                            masked_decays(g + 1, 0)
                        dve.wait_ge(og_e, n(og_e))
                        seg = hp[:, 512 * m:512 * m + 512].rearrange("p (c n) -> p c n", c=4)
                        cb = xt[:, 256 * (g % 2) + T * P:256 * (g % 2) + T * P + P]
                        dve.tensor_tensor(seg, seg, bc_mid(cb, 4), ALU.mult).then_inc(og_m, 1)
                        if m:
                            x = o_x[:, T, cols]
                            link(dve.tensor_tensor(eight(x), eight(x), bc(m_dskip[:, 8 * g:8 * g + 8], C_DIM), ALU.mult))
                            dve.wait_ge(og_y, n(og_y, 2))
                            link(dve.tensor_tensor(x, x, ps[:, 4 + T, :], ALU.add))
                            if T:
                                dve.wait_ge(og_off, n(og_off))
                                off = xt[:, 1024:1536]
                                link(dve.tensor_tensor(eight(off), eight(ps[:, 7, :]), bc(of(T_ECUM, 1, g), C_DIM), ALU.mult))
                                link(dve.tensor_tensor(x, x, off, ALU.add))
                            dve.tensor_tensor(o_z[:, T, cols], o_z[:, T, cols], x, ALU.mult).then_inc(og_yz, 1)
                dve.wait_ge(sq_done, n(sq_done))
                inverse_rms(8, C_GROUPS / C_INNER)
                for T in range(TB):
                    y = o_z[:, T, :].rearrange("p (g n) -> p g n", g=C_GROUPS)
                    dve.tensor_tensor(y, y, bc(rstd[:, 4 * T:4 * T + 4], BANK), ALU.mult).then_inc(xn_done, 1)
                split_act(rounds=2, scale=lambda c: colv[:, V_OON + c:V_OON + c + 1])
                split(8)

            def mod_columns(l, half):
                dve.wait_ge(mod_col, n(mod_col))
                at_col, v = 24 * half, V_ADAB + 48 * l + 24 * half
                link(dve.tensor_tensor(modv[:, at_col:at_col + 24], ps[:, 4 + half, at_col:at_col + 24], colv[:, v:v + 24], ALU.add))
                a, g = modv[:, at_col + 8:at_col + 16], (V_N2 if half else V_N1) + 8 * l
                link(dve.scalar_tensor_tensor(a, a, 1.0, colv[:, g:g + 8], ALU.add, ALU.mult))
                if l == 0 and half == 0:
                    link(dve.tensor_tensor(modc, ps[:, 4, 48:64], colv[:, V_ADAB:V_ADAB + 16], ALU.add))
                    a = modc[:, MOD_A1:MOD_A1 + 8]
                    link(dve.scalar_tensor_tensor(a, a, 1.0, colv[:, V_N1:V_N1 + 8], ALU.add, ALU.mult))

            def mod(at_col, m=None):
                return lambda c: (modv if m is None else m)[:, at_col + c:at_col + c + 1]

            def add_branch():
                row_copy()
                dve.wait_ge(gran_used, 2 * at[0])
                for tb in range(TB):
                    link(dve.tensor_tensor(xn[:, tb, :], banks(2 * tb, 2), wbc[:], ALU.mult))
                    dve.tensor_tensor(h[:, tb, :], h[:, tb, :], xn[:, tb, :], ALU.add).then_inc(h_ready if tb else h_first, 1)
                if at[0] + 2 <= moe_from:
                    split_ahead(1)

            def diff_attention():
                dots = hp[:, 0:128].rearrange("p (k n) -> p k n", k=2)
                link(dve.tensor_tensor(dots, m_lq[:, 0:4:2, :], m_lq[:, 1:4:2, :], ALU.mult))
                dve.tensor_reduce(w8(44, 2), dots, AX_X, ALU.add).then_inc(sv_in, 1)
                dve.tensor_scalar(w8(45, 1), colv[:, V_SUBLN:V_SUBLN + 1], 1.0 - LAM_INIT, None, ALU.mult)
                split(12)
                for c in range(8):
                    dve.wait_ge(da_kt, n(da_kt))
                    dve.tensor_copy(da_kT[:, c, :], ps[:, 4 + c % 4, :]).then_inc(da_kc, 1)
                dve.wait_ge(sv_out, n(sv_out))
                minus_lam = w8(46, 1)
                link(dve.tensor_tensor(minus_lam, w8(43, 2)[:, 1:2], w8(43, 2)[:, 0:1], ALU.subtract))
                link(dve.tensor_scalar(minus_lam, minus_lam, -LAM_INIT, None, ALU.add))

                def maxima(u):
                    dve.wait_ge(da_s, n(da_s))
                    m = w8(40)[:, 2 * (u % 2):2 * (u % 2) + 2]
                    link(dve.tensor_reduce(m, ps[:, 2 * (u % 2):2 * (u % 2) + 2, :], AX_X, ALU.max))
                    dve.tensor_scalar(m, m, -DA_DIM ** -0.5, None, ALU.mult).then_inc(da_m, 1)

                units = TB * DA_HEADS
                maxima(0)
                maxima(1)
                for u in range(units):
                    dve.wait_ge(da_e, n(da_e))
                    if u >= 2:
                        dve.wait_ge(da_at, u - 1)
                    r = w8(42)[:, 2 * (u % 2):2 * (u % 2) + 2]
                    a, e = wbc[:, 512 * (u % 2):512 * (u % 2) + 512], xt[:, 1024 * (u % 2):1024 * (u % 2) + 1024]
                    link(dve.reciprocal(r, w8(41)[:, 2 * (u % 2):2 * (u % 2) + 2]))
                    dve.tensor_scalar(r[:, 1:2], r[:, 1:2], minus_lam, None, ALU.mult)
                    link(dve.tensor_scalar(a, e[:, 0:512], r[:, 0:1], None, ALU.mult))
                    dve.scalar_tensor_tensor(a, e[:, 512:1024], r[:, 1:2], a, ALU.mult, ALU.add).then_inc(da_a, 1)
                    if u + 2 < units:
                        maxima(u + 2)
                dve.wait_ge(da_oc, units)
                inverse_rms(16, 1.0 / P)
                for tb in range(TB):
                    v = xn[:, tb, :].rearrange("p (c n) -> p c n", c=DC)
                    scaled(v, v, rstd[:, 8 * tb:8 * tb + 8]).then_inc(xn_done, 1)
                split_act(scale=lambda c: w8(45, 1))
                split(4)

            def fourier():
                dve.tensor_tensor(hp[:].rearrange("p (c n) -> p c n", c=DC), bc_mid(ident, DC), bc(colv[:, V_FNB:V_FNB + 8], P),
                                  ALU.mult).then_inc(diag_done, 1)
                dve.wait_ge(sq_done, n(sq_done, TB))
                inverse_rms(TB, 1.0 / DM)
                for tb in range(TB):
                    dve.tensor_scalar(xn[:, tb, :], h[:, tb, :], rstd[:, tb:tb + 1], None, ALU.mult).then_inc(xn_done, 1)
                for b in range(4):
                    dve.wait_ge(tp_done, n(tp_done))
                    for c in (2 * b, 2 * b + 1):
                        ins = dve.tensor_scalar(xt[:, c * TOKENS:(c + 1) * TOKENS], ps[:, b, (c % 2) * TOKENS:(c % 2 + 1) * TOKENS],
                                                mod(MOD_A1)(c), mod(MOD_B1)(c), ALU.mult, ALU.add)
                    ins.then_inc(xt_done, 1)
                dve.wait_ge(ft_x, n(ft_x, 8))
                split_act()
                split(4)

            def experts():
                def row_out(dst):
                    dve.wait_ge(bc_ready, n(bc_ready))
                    dve.tensor_copy(dst, banks(6, 2)).then_inc(row_read, 1)

                dve.tensor_tensor(hp[:].rearrange("p (c n) -> p c n", c=DC), bc_mid(ident, DC), bc(colv[:, V_FIN:V_FIN + 8], P),
                                  ALU.mult).then_inc(diag_done, 1)
                mod_columns(1, 1)
                row_diag(modv[:, MOD_G2:MOD_G2 + 8])
                dve.tensor_scalar(r_rev, iota[:, P:P + 8], -1.0, float(N_EXPERTS), ALU.mult, ALU.add)
                dve.memset(r_tab[:, :, 11:12], 0.0)
                dve.memset(mo_PT, 0.0).then_inc(mo_ptc, 1)
                row_out(fin_g)
                dve.wait_ge(sq_done, n(sq_done, TB))
                inverse_rms(TB, 1.0 / DM)
                for tb in range(TB):
                    dve.tensor_scalar(xn[:, tb, :], h[:, tb, :], rstd[:, tb:tb + 1], None, ALU.mult).then_inc(xn_done, 1)
                for b in range(4):
                    dve.wait_ge(tp_done, n(tp_done))
                    for c in (2 * b, 2 * b + 1):
                        ins = dve.tensor_scalar(xt[:, c * TOKENS:(c + 1) * TOKENS], ps[:, b, (c % 2) * TOKENS:(c % 2 + 1) * TOKENS],
                                                mod(MOD_A2)(c), mod(MOD_B2)(c), ALU.mult, ALU.add)
                    ins.then_inc(xt_done, 1)
                row_out(wbc[:])
                dve.memset(mo_acc, 0.0)

                dve.wait_ge(mo_lg, n(mo_lg))
                link(dve.tensor_copy(r_lg, ps[:, 4, 0:16].rearrange("p (b e) -> p b e", b=TB)))

                def best(value, oh):
                    link(dve.tensor_reduce(value, r_lg, AX_X, ALU.max))
                    link(dve.tensor_tensor(r_tmp, r_lg, bc(value, 8), ALU.is_ge))
                    link(dve.tensor_tensor(r_tmp, r_tmp, bc_mid(r_rev, TB), ALU.mult))
                    link(dve.tensor_reduce(r_g1, r_tmp, AX_X, ALU.max))
                    link(dve.tensor_tensor(oh, bc_mid(r_rev, TB), bc(r_g1, 8), ALU.is_equal))

                best(r_v1, r_oh1)
                link(dve.scalar_tensor_tensor(r_lg, r_oh1, NEG, r_lg, ALU.mult, ALU.add))
                best(r_v2, r_oh2)
                dve.tensor_tensor(r_q[:, R_SEL:R_SEL + 2, :], r_oh1, r_oh2, ALU.add).then_inc(mo_sel, 1)
                dve.tensor_tensor(r_d, r_v2, r_v1, ALU.subtract).then_inc(mo_v, 1)
                dve.wait_ge(mo_ex, n(mo_ex))
                link(dve.tensor_scalar(r_g1, r_e, 1.0, None, ALU.add))
                link(dve.reciprocal(r_g1, r_g1))
                link(dve.tensor_tensor(r_g2, r_g1, r_e, ALU.mult))
                dve.tensor_tensor(r_oh1, r_oh1, bc(r_g1, 8), ALU.mult)
                link(dve.tensor_tensor(r_oh2, r_oh2, bc(r_g2, 8), ALU.mult))
                dve.tensor_tensor(r_q[:, R_GATE:R_GATE + 2, :], r_oh1, r_oh2, ALU.add)
                def places(b):
                    for tb in range(TB):
                        def of(q):
                            return r_tab[:, q + tb, bass.ds(b, 1)]
                        ins = dve.tensor_scalar(mo_P[:, tb, :], iota[:, 0:P], of(R_RANK), of(R_SEL), ALU.is_equal, ALU.mult)
                    ins.then_inc(mo_link, 1)
                    dve.wait_ge(mo_link, n(mo_link))
                    for tb in range(TB):
                        ins = dve.tensor_scalar(mo_PG[:, tb, :], mo_P[:, tb, :], r_tab[:, R_GATE + tb, bass.ds(b, 1)], None, ALU.mult)
                    ins.then_inc(mo_p, 1)

                def gather_out():
                    for k in range(2):
                        dve.wait_ge(mo_x, n(mo_x))
                        for c in range(4):
                            cols = slice(c * P, (c + 1) * P)
                            ins = dve.tensor_scalar(mo_xe[k][:, cols], ps[:, 5 + 2 * k, cols],
                                                    mod(MOD_A2)(4 * k + c), mod(MOD_B2)(4 * k + c), ALU.mult, ALU.add)
                        ins.then_inc(mo_xc, 1)

                def gathered():
                    for k in range(2):
                        dve.wait_ge(mo_xh, n(mo_xh))
                        dve.tensor_tensor(act_lo[:, 4 * k:4 * k + 4, 0:P], mo_xe[k].rearrange("p (c n) -> p c n", c=4),
                                          act_hi[:, 4 * k:4 * k + 4, 0:P].bitcast(F32), ALU.subtract).then_inc(mo_xl, 1)

                def add_spread():
                    dve.tensor_tensor(mo_acc[:, 0, :], mo_acc[:, 0, :], banks(2, 2), ALU.add)
                    for nh in range(2):
                        half = mo_acc[:, 1, nh * BANK:(nh + 1) * BANK]
                        ins = dve.tensor_tensor(half, half, ps[:, 5 + 2 * nh, :], ALU.add)
                    return ins

                dve.wait_ge(mo_rank, n(mo_rank))
                link(dve.tensor_copy(r_q[:, R_RANK:R_RANK + 2, :], ps[:, 4, 16:32].rearrange("p (b e) -> p b e", b=TB)))
                link(dve.tensor_copy(r_tab[:, :, 0:8], r_q))
                places(0)
                link(dve.tensor_scalar(r_cnt, ps[:, 4, 32:40], P + 0.5, None, ALU.is_ge))
                dve.tensor_copy(r_ids[:, 0:8], iota[:, P:P + 8])
                link(dve.tensor_reduce(r_ids[:, 11:12], r_cnt, AX_X, ALU.add))
                dve.tensor_scalar(r_ids[:, 11:12], r_ids[:, 11:12], float(N_EXPERTS), None, ALU.add)
                link(dve.tensor_tensor(r_code, r_cnt, r_rev, ALU.mult))
                for k in range(MAX_EXTRA):
                    link(dve.tensor_reduce(r_ck[:, k:k + 1], r_code, AX_X, ALU.max))
                    dve.tensor_scalar(r_ohk[:, k, :], r_rev, r_ck[:, k:k + 1], None, ALU.is_equal)
                    link(dve.scalar_tensor_tensor(r_code, r_code, r_ck[:, k:k + 1], r_code, ALU.is_lt, ALU.mult))
                link(dve.tensor_scalar(r_ids[:, 8:11], r_ck, -1.0, float(N_EXPERTS), ALU.mult, ALU.add))
                link(dve.tensor_scalar(r_ids[:, 8:11], r_ids[:, 8:11], N_EXPERTS - 1.0, None, ALU.min))
                dve.tensor_copy(eid[:], r_ids[0:1, :]).then_inc(mo_ids, 1)
                gather_out()
                gathered()
                for k in range(MAX_EXTRA):
                    link(dve.tensor_tensor(r_t48, r_q, bc_mid(r_ohk[:, k, :], 6), ALU.mult))
                    link(dve.tensor_reduce(r_tab[:, :, 8 + k:9 + k], r_t48, AX_X, ALU.add))
                    link(dve.tensor_scalar(r_tab[:, R_RANK:R_RANK + 2, 8 + k:9 + k], r_tab[:, R_RANK:R_RANK + 2, 8 + k:9 + k],
                                           -float(P), None, ALU.add))
                dve.wait_ge(mo_ids, 1)
                n_blocks = dve.value_load(eid[0:1, 11:12], min_val=N_EXPERTS, max_val=N_EXPERTS + MAX_EXTRA)
                with dve.Fori(0, n_blocks) as b:
                    start_blocks(n, b)

                    def beside(i):
                        if i == ADDED_AT:
                            dve.wait_ge(mo_c, n(mo_c))
                            add_spread().then_inc(mo_cc, 1)
                        if i == PLACES_AT:
                            dve.wait_ge(mo_pt, n(mo_pt))
                            places(b + 1)
                        if i == GATHERED_AT:
                            gather_out()
                        if i == FF_STEPS:
                            gathered()
                    gated(FF2, 1, beside)
                    end_blocks(n)
                dve.wait_ge(mo_end_c, n(mo_end_c))
                add_spread()
                dve.tensor_copy(r_v1, r_v2).then_inc(fin_link, 1)
                dve.wait_ge(fin_link, 1)
                for tb in range(TB):
                    ins = dve.tensor_tensor(mo_acc[:, tb, :], mo_acc[:, tb, :], wbc[:], ALU.mult)
                ins.then_inc(fin_link, 1)
                dve.wait_ge(fin_link, 2)
                dve.tensor_tensor(h[:], h[:], mo_acc, ALU.add).then_inc(h_ready, 1)
                dve.wait_ge(sq_done, n(sq_done, TB))
                inverse_rms(TB, 1.0 / DM)
                for tb in range(TB):
                    dve.scalar_tensor_tensor(xn[:, tb, :], h[:, tb, :], rstd[:, tb:tb + 1], fin_g, ALU.mult, ALU.mult).then_inc(fin, 1)

            dve.wait_ge(rows_t, n(rows_t))
            link(dve.tensor_copy(colv[:, 0:ROWS_A], ps[:, 0, 0:ROWS_A]))
            link(dve.tensor_copy(colv[:, P:P + 96], ps[:, 1, 0:96]))
            link(dve.tensor_copy(colv[:, 2 * P:3 * P], ps[:, 2, 0:P]))
            link(dve.tensor_copy(colv[:, V_ADAB:V_ADAB + 96], ps[:, 3, 0:96]))
            norm(lambda c: nw(0, 0)[:, c:c + 1])
            gated(FF1)
            residual(nw(0, 1), 0.5)
            norm(lambda c: nw(0, 2)[:, c:c + 1])
            even()
            residual(nw(0, 3), 1.0)
            norm(lambda c: nw(0, 4)[:, c:c + 1])
            gated(FF1)
            residual(nw(0, 5), 0.5)
            norm(lambda c: nw(1, 0)[:, c:c + 1])
            gated(FF1)
            residual(nw(1, 1), 0.5)
            mod_columns(0, 0)
            mod_columns(0, 1)
            norm(lambda c: nw(1, 2)[:, c:c + 1])
            odd()
            residual(nw(1, 3), 1.0)
            norm(lambda c: nw(1, 4)[:, c:c + 1])
            gated(FF1)
            residual(nw(1, 5), 0.5)
            norm(mod(MOD_A1), mod(MOD_B1))
            norm(mod(MOD_A1, modc), mod(MOD_B1, modc), src=ctx_x, base=8)
            diff_attention()
            row_diag(modv[:, MOD_G1:MOD_G1 + 8])
            add_branch()
            norm(mod(MOD_A2), mod(MOD_B2))
            gated(FF2)
            row_diag(modv[:, MOD_G2:MOD_G2 + 8])
            add_branch()
            mod_columns(1, 0)
            fourier()
            row_diag(modv[:, MOD_G1:MOD_G1 + 8])
            add_branch()
            experts()

        @block.tensor
        def _(pe):
            n = Count()
            at = [0]

            def three(out_ap, chunk, cols, g, o, width, start, stop):
                hi, lo = act_hi[:, chunk, cols], act_lo[:, chunk, cols]
                whi, wlo = w_hi[:, g % SPLITS, o:o + width], w_lo[:, g % SPLITS, o:o + width]
                pe.matmul(out_ap, hi, whi, start=start, stop=False)
                pe.matmul(out_ap, lo, whi, start=False, stop=False)
                return pe.matmul(out_ap, hi, wlo, start=False, stop=stop)

            def up(k, outs, alo_before=None):
                last = sum(slots[s][1] for s in range(at[0], at[0] + k))
                chunk = 0
                for s in range(at[0], at[0] + k):
                    for j in range(2):
                        g = 2 * s + j
                        c, width, _ = granule(s, j)
                        pe.wait_ge(lo_done, n.gran(g + 1))
                        for i in range(c):
                            if alo_before is not None and chunk % 2 == 0:
                                pe.wait_ge(alo_done, alo_before + chunk // 2 + 1)
                            for base, cols, bank in outs:
                                ins = three(ps[:, bank, 0:width], base + chunk, cols, g, i * width, width,
                                            chunk == 0, chunk == last - 1)
                            chunk += 1
                        ins.then_inc(gran_used, 1)
                at[0] += k

            def down(k, base, first, final, tbs=TB):
                chunk = 0
                for s in range(at[0], at[0] + k):
                    for j in range(2):
                        g = 2 * s + j
                        pe.wait_ge(lo_done, n.gran(g + 1))
                        for tb in range(tbs):
                            for nh in range(2):
                                ins = three(ps[:, 2 * tb + nh, :], base + chunk, slice(tb * P, tb * P + P), g, nh * BANK, BANK,
                                            first and chunk == 0, final and chunk == 2 * k - 1)
                        chunk += 1
                        ins.then_inc(gran_used, 1)
                at[0] += k

            def transposes(src, rounds=1):
                for r in range(rounds):
                    for b in range(4):
                        if r:
                            pe.wait_ge(xt_done, n(xt_done))
                        for c in (2 * b, 2 * b + 1):
                            for tb in range(TB):
                                ins = pe.transpose(ps[:, b, (c % 2) * TOKENS + tb * P:(c % 2) * TOKENS + tb * P + P],
                                                   src[:, tb, (8 * r + c) * P:(8 * r + c + 1) * P], ident)
                        ins.then_inc(tp_done, 1)
                n(xt_done, 4)

            def norm(lead=False):
                pe.wait_ge(xn_done, n(xn_done, TB))
                transposes(xn)
                n(alo_done, 4)
                if not lead:
                    pe.wait_ge(alo_done, n.last(alo_done))

            def gated(ff, tbs=TB, beside=None):
                s = steps(ff)
                blocks = [slice(tb * P, tb * P + P) for tb in range(tbs)]

                def hidden(i):
                    c = s[i][1] // P
                    pe.wait_ge(hid_done, n(hid_done))
                    for k in range(c):
                        for tb in range(tbs):
                            o = (k * tbs + tb) * P
                            ins = pe.transpose(banks(6, tbs)[:, o:o + P], hp[:, tb * BANK + k * P:tb * BANK + k * P + P], ident)
                    ins.then_inc(hid_t, 1)

                for i, (_, width) in enumerate(s):
                    per = 2 if width == BANK else 1
                    if i:
                        pe.wait_ge(silu_done, n(silu_done))
                    up(per, [(0, b, 4 + k) for k, b in enumerate(blocks)],
                       n.last(alo_done, 4) if i == 0 and tbs == TB else None)
                    if i:
                        pe.wait_ge(hid_x, n(hid_x))
                    up(per, [(0, b, 6 + k) for k, b in enumerate(blocks)])
                    if beside:
                        beside(i)
                    if i:
                        pe.wait_ge(hlo_done, n(hlo_done))
                        down(2 if s[i - 1][1] == BANK else 1, 8 + 4 * ((i - 1) % 2), i == 1, False, tbs)
                    hidden(i)
                n(silu_done)
                pe.wait_ge(hid_x, n(hid_x))
                pe.wait_ge(hlo_done, n(hlo_done))
                down(2 if s[-1][1] == BANK else 1, 8 + 4 * ((len(s) - 1) % 2), len(s) == 1, True, tbs)

            def row_broadcast():
                pe.wait_ge(diag_done, n(diag_done))
                for i in range(2):
                    ins = pe.matmul(ps[:, 6 + i, :], ones, sg[:, i * BANK:(i + 1) * BANK], start=True, stop=True)
                ins.then_inc(bc_ready, 1)

            def even():
                blocks = [slice(tb * P, tb * P + P) for tb in range(TB)]
                for j in range(8):
                    if j >= 4:
                        pe.wait_ge(proj_out, n(proj_out))
                    up(2 if j < 7 else 1, [(0, b, 2 * (j % 4) + k) for k, b in enumerate(blocks)])
                pe.wait_ge(proj_out, n(proj_out, 4))
                for i in range(4):
                    for c in range(2):
                        for tb in range(TB):
                            at_c = (2 * (i % 2) + c) * P
                            ins = pe.transpose(ps[:, 4 + i, c * TOKENS + tb * P:c * TOKENS + tb * P + P],
                                               e_qkv[:, i // 2, tb, at_c:at_c + P], ident)
                    ins.then_inc(qk_tp, 1)

                def to_convolve(f):
                    for c in (2 * f, 2 * f + 1):
                        for tb in range(TB):
                            o = (c % 2) * TOKENS + tb * P
                            ins = pe.transpose(ps[:, f % 2, o:o + P], e_raw[:, tb, c * P:(c + 1) * P], ident)
                    ins.then_inc(cv_tp, 1)

                def scores(i):
                    r, c = slice((i % 2) * A_DIM, (i % 2 + 1) * A_DIM), i // 2
                    pe.matmul(ps[:, 4 + i % 2, 0:P], e_qt[r, c, 0:P], e_kt[r, c, 0:P], start=True, stop=True)
                    pe.matmul(ps[:, 4 + i % 2, P:384], e_qt[r, c, P:TOKENS], e_kt[r, c, :], start=True, stop=True).then_inc(at_sc, 1)

                for f in range(6):
                    if f >= 2:
                        pe.wait_ge(cv_done, n(cv_done))
                    to_convolve(f)
                pe.wait_ge(qk_cp, n(qk_cp, 4))
                n(cv_done, 2)
                scores(0)
                for i in range(A_HEADS):
                    if i + 1 < A_HEADS:
                        scores(i + 1)
                    pe.wait_ge(at_p, n(at_p))
                    for k in range(3):
                        ins = pe.transpose(ps[:, 6 + i % 2, k * P:(k + 1) * P], a_p[:, i % 2, k * P:(k + 1) * P], ident)
                    ins.then_inc(at_pt, 1)
                    pe.wait_ge(at_pc, n(at_pc))
                    if i >= 2:
                        pe.wait_ge(at_o, n(at_o))
                    o = ps[:, 2 + i % 2, :]
                    v = e_qkv[:, 2, :, i * A_DIM:(i + 1) * A_DIM]
                    pe.matmul(o[:, 0:A_DIM], a_pt[:, i % 2, 0:P], v[:, 0, :], start=True, stop=True)
                    pe.matmul(o[:, A_DIM:2 * A_DIM], a_pt[:, i % 2, P:2 * P], v[:, 0, :], start=True, stop=False)
                    pe.matmul(o[:, A_DIM:2 * A_DIM], a_pt[:, i % 2, 2 * P:3 * P], v[:, 1, :], start=False, stop=True).then_inc(at_pv, 1)
                n(at_o, 2)
                pe.wait_ge(dl_g, n(dl_g))
                pe.matmul(ps[:, 0, 0:8], tri, w8(1), start=True, stop=True)
                pe.matmul(ps[:, 0, 8:16], ones, w8(1), start=True, stop=True)
                pe.matmul(ps[:, 1, 0:P], ones, sg[:, 0:P], start=True, stop=True).then_inc(dl_gc, 1)
                pe.wait_ge(cv_act, n(cv_act, 6))
                pe.wait_ge(sv_in, n(sv_in, 2))

                for T in range(TB):
                    def each(bank, fn):
                        for i in range(B_HEADS):
                            ins = fn(i, ps[:, bank, i * P:(i + 1) * P])
                        return ins

                    def product(a, b):
                        return lambda i, o: pe.matmul(o, a[:, i, :], b[:, i, :], start=True, stop=True)

                    for b in range(3):
                        each(b, lambda i, o: pe.transpose(o, e_cv[:, 4 * b + i, T * P:(T + 1) * P], ident)).then_inc(dl_tm, 1)
                    pe.wait_ge(dl_in, n(dl_in))
                    for b, src in enumerate((d_tm[:, 0:4, :], d_tm[:, 4:8, :], d_kb, d_qd)):
                        each(3 + b, lambda i, o: pe.transpose(o, src[:, i, :], ident)).then_inc(dl_t3, 1)
                    pe.wait_ge(dl_lg, n(dl_lg))
                    pe.matmul(ps[:, 7, :], ident, bc_mid(neg, 4), start=True, stop=False)
                    pe.matmul(ps[:, 7, :], ones, d_A.rearrange("p c n -> p (c n)"), start=False, stop=True).then_inc(dl_R, 1)
                    pe.wait_ge(dl_tc, n(dl_tc, 4))
                    each(0, product(d_kT, d_kbT))
                    each(1, product(d_kT, d_qT)).then_inc(dl_at, 1)
                    pe.wait_ge(dl_xt, n(dl_xt))
                    each(2, lambda i, o: pe.transpose(o, d_XT[:, i, :], ident)).then_inc(dl_xtt, 1)
                    for level in range(1, 7):
                        pe.wait_ge(dl_off, n(dl_off))
                        pe.wait_ge(dl_x, n(dl_x))
                        each(3, product(d_off[level % 2], d_X)).then_inc(dl_y, 1)
                        pe.wait_ge(dl_yc, n(dl_yc))
                        ins = each(4, product(d_Y, d_XT))
                        if level < 6:
                            ins = each(5, product(d_XT, d_Y))
                        ins.then_inc(dl_xy, 1)
                    pe.wait_ge(dl_x, n(dl_x))
                    ins = each(6, product(d_XT, d_tm[:, 8:12, :]))
                    if T:
                        ins = each(7, product(d_kbg, d_XT))
                    ins.then_inc(dl_u, 1)
                    if T:
                        pe.wait_ge(dl_uc, n(dl_uc))
                        each(2, product(d_kT, d_S)).then_inc(dl_ws, 1)
                        pe.wait_ge(dl_vn, n(dl_vn))
                        for i in range(B_HEADS):
                            o = ps[:, 0, i * P:(i + 1) * P]
                            pe.matmul(o, d_qdT[:, i, :], d_S[:, i, :], start=True, stop=False)
                            ins = pe.matmul(o, d_QK[:, i, :], d_kbT[:, i, :], start=False, stop=True)
                        ins.then_inc(dl_o, 1)
                    else:
                        pe.wait_ge(dl_vn, n(dl_vn))
                        each(0, product(d_QK, d_kbT))
                        each(1, product(d_kd, d_kbT)).then_inc(dl_o, 1)
                        pe.wait_ge(xn_done, n(xn_done))
                pe.wait_ge(xn_done, n(xn_done))
                transposes(xn)
                pe.wait_ge(alo_done, n(alo_done, 4))
                down(4, 0, True, True)
                row_broadcast()

            def odd():
                blocks = [slice(tb * P, tb * P + P) for tb in range(TB)]
                for j in range(13):
                    if j < 11:
                        if j >= 2:
                            pe.wait_ge(proj_out, n(proj_out))
                        up(2 if j < 10 else 1, [(0, b, 2 * (j % 2) + k) for k, b in enumerate(blocks)])
                    if 4 <= j - 1 < 10:
                        if j == 5:
                            pe.wait_ge(proj_out, 8 + 5)
                        elif j < 11:
                            pe.wait_ge(proj_out, 8 + j)
                        if j > 5:
                            pe.wait_ge(cv_done, n(cv_done, 2))
                        for f in range(2):
                            for c in range(2):
                                for tb in range(TB):
                                    o = c * TOKENS + tb * P
                                    at_c = tb * BANK + (2 * f + c) * P
                                    ins = pe.transpose(ps[:, 4 + f, o:o + P], xn[:, (j - 1) % 2, at_c:at_c + P], ident)
                            ins.then_inc(cv_tp, 1)
                    if 4 <= j - 3 < 9:
                        pe.wait_ge(cv_act, n(cv_act, 2))
                        if j > 7:
                            pe.wait_ge(o_tc, n(o_tc))
                        half = 1024 * ((j - 1) % 2)
                        for tb in range(TB if j - 3 < 8 else 1):
                            for c in range(4):
                                src = xt[:, half + c * TOKENS + tb * P:half + c * TOKENS + tb * P + P] if j - 3 < 8 else o_bc[:, c, 0:P]
                                ins = pe.transpose(ps[:, 6 + tb, c * P:(c + 1) * P], src, ident)
                        ins.then_inc(o_tp, 1)
                n(cv_done, 2)
                n(o_tc)
                n(proj_out, 2)
                pe.wait_ge(cv_act, n(cv_act, 2))
                pe.wait_ge(dl_g, n(dl_g))
                pe.matmul(ps[:, 0, 0:64], tri, dtw[:, T_A, :], start=True, stop=True)
                pe.matmul(ps[:, 0, 64:128], ones, dtw[:, T_A, :], start=True, stop=True).then_inc(dl_gc, 1)
                pe.wait_ge(sv_in, n(sv_in, 2))

                def rows(m):
                    pe.wait_ge(og_la, n(og_la))
                    pe.matmul(ps[:, 2 + m, :], ident, bc_mid(neg, 4), start=True, stop=False)
                    pe.matmul(ps[:, 2 + m, :], ones, sg[:, 512 * m:512 * m + 512], start=False, stop=True).then_inc(og_R, 1)

                rows(0)
                for g in range(C_GROUPS):
                    for T in range(TB):
                        tok = slice(T * P, T * P + P)
                        ins = pe.matmul(ps[:, 0, tok], o_bc[:, g, tok], o_bc[:, 4 + g, tok], start=True, stop=True)
                    ins.then_inc(og_cb, 1)
                    pe.wait_ge(og_x, n(og_x))
                    pe.matmul(ps[:, 6, :], o_bt[:, g, :], o_xd, start=True, stop=True).then_inc(og_s, 1)
                    for q in range(4):
                        T, m = q // 2, q % 2
                        if q < 3 or g < 3:
                            rows(1 - m)
                        pe.wait_ge(og_m, n(og_m))
                        if g and not m:
                            pe.wait_ge(og_yz, n(og_yz))
                        for i in range(4):
                            o = 256 * m + i * C_DIM
                            ins = pe.matmul(ps[:, 4 + T, o:o + C_DIM], hp[:, 512 * m + i * P:512 * m + (i + 1) * P],
                                            o_xdt[:, T, o:o + C_DIM], start=True, stop=True)
                        ins.then_inc(og_y, 1)
                        if q == 2:
                            pe.wait_ge(og_sc, n(og_sc))
                            pe.matmul(ps[:, 7, :], o_bc[:, 4 + g, P:TOKENS], o_st, start=True, stop=True).then_inc(og_off, 1)
                n(og_yz, 2)
                pe.wait_ge(xn_done, n(xn_done, 2))
                transposes(o_z, rounds=2)
                pe.wait_ge(alo_done, n(alo_done, 8))
                down(8, 0, True, True)
                row_broadcast()

            def mod_columns(l, half):
                context = l == 0 and half == 0
                for nb in range(3 * half, 3 * half + 3):
                    n(ada_sum, 16 if context and nb < 2 else 8)
                pe.wait_ge(ada_sum, n.last(ada_sum))
                for k in range(24 * half, 24 * half + 24):
                    ins = pe.matmul(ps[:, 4 + half, k:k + 1], m_sum[:, k * P:(k + 1) * P], ones[:, 0:1], start=True, stop=True)
                if context:
                    for k in range(16):
                        ins = pe.matmul(ps[:, 4, 48 + k:49 + k], m_sumc[:, k * P:(k + 1) * P], ones[:, 0:1], start=True, stop=True)
                ins.then_inc(mod_col, 1)

            def diff_attention():
                rows = [slice(tb * P, tb * P + P) for tb in range(TB)]
                for j in range(6):
                    b = 4 * (j % 2)
                    if j >= 2:
                        pe.wait_ge(proj_out, 19 + j - 1)
                    if j < 2:
                        up(2, [(0, rows[0], b), (0, rows[1], b + 1)])
                    else:
                        up(2, [(8, rows[0], b), (8, rows[1], b + 1), (0, rows[0], b + 2), (0, rows[1], b + 3)])
                pe.wait_ge(proj_out, 19 + 5)
                pe.wait_ge(rope_done, 1)
                for b in range(4):
                    for c in (2 * b, 2 * b + 1):
                        for tb in range(TB):
                            o = (c % 2) * TOKENS + tb * P
                            ins = pe.transpose(ps[:, b, o:o + P], xn[:, tb, c * P:(c + 1) * P], ident)
                    ins.then_inc(da_qt, 1)
                pe.wait_ge(proj_out, 19 + 6)
                pe.wait_ge(rope_done, 2)
                for c in range(8):
                    if c >= 4:
                        pe.wait_ge(da_kc, c - 3)
                    for tb in range(4):
                        ins = pe.transpose(ps[:, 4 + c % 4, tb * P:(tb + 1) * P], da_k[:, tb, c * P:(c + 1) * P], ident)
                    ins.then_inc(da_kt, 1)

                def scores(u):
                    head, tb = u // 2, u % 2
                    for k in range(2):
                        r = slice(k * DA_DIM, (k + 1) * DA_DIM)
                        ins = pe.matmul(ps[:, 2 * (u % 2) + k, :], da_qT(head)[r, tb * P:(tb + 1) * P], da_kT[r, head, :],
                                        start=True, stop=True)
                    ins.then_inc(da_s, 1)

                units = TB * DA_HEADS
                pe.wait_ge(da_qc, 4)
                pe.wait_ge(da_kc, 8)
                scores(0)
                scores(1)
                for u in range(units):
                    pe.wait_ge(da_a, n(da_a))
                    for kb in range(4):
                        ins = pe.transpose(ps[:, 4 + u % 2, kb * P:(kb + 1) * P], wbc[:, 512 * (u % 2) + kb * P:512 * (u % 2) + (kb + 1) * P], ident)
                    ins.then_inc(da_at, 1)
                    if u + 2 < units:
                        scores(u + 2)
                    pe.wait_ge(da_ac, n(da_ac))
                    if u >= 2:
                        pe.wait_ge(da_oc, u - 1)
                    head = u // 2
                    for kb in range(4):
                        ins = pe.matmul(ps[:, 6 + u % 2, 0:P], da_aT[:, u % 2, kb * P:(kb + 1) * P], da_v[:, kb, head * P:(head + 1) * P],
                                        start=kb == 0, stop=kb == 3)
                    ins.then_inc(da_o, 1)
                pe.wait_ge(xn_done, n(xn_done, TB))
                transposes(xn)
                pe.wait_ge(alo_done, n(alo_done, 4))
                down(4, 0, True, True)
                row_broadcast()

            def fourier():
                pe.wait_ge(xn_done, n(xn_done, TB))
                transposes(xn)
                pe.wait_ge(tab_in, 64)
                pe.wait_ge(xt_done, n.last(xt_done))
                for g in range(8):
                    for tb in range(TB):
                        ins = pe.matmul(ps[:, g, tb * TOKENS:(tb + 1) * TOKENS], xt[:, g * TOKENS + tb * P:g * TOKENS + tb * P + P], f_g,
                                        start=True, stop=True)
                    ins.then_inc(ft_x, 1)
                pe.wait_ge(ft_c, 8)
                for g in range(8):
                    for i in range(4):
                        k, tb = divmod(i, 2)
                        ins = pe.matmul(ps[:, g // 2, (g % 2) * TOKENS:(g % 2 + 1) * TOKENS], f_z(g)[:, tb, k * P:(k + 1) * P],
                                        f_l[:, k, tb, :], start=i == 0, stop=i == 3)
                    if g % 2:
                        ins.then_inc(tp_done, 1)
                n(xt_done, 4)
                pe.wait_ge(alo_done, n(alo_done, 4))
                pe.wait_ge(diag_done, n(diag_done))
                for tb in range(TB):
                    for nh in range(2):
                        pe.matmul(ps[:, 2 * tb + nh, :], ones, hp[:, nh * BANK:(nh + 1) * BANK], start=True, stop=False)
                down(4, 0, False, True)
                row_broadcast()

            def experts():
                mod_columns(1, 1)
                pe.wait_ge(diag_done, n(diag_done))
                for i in range(2):
                    ins = pe.matmul(ps[:, 6 + i, :], ones, hp[:, i * BANK:(i + 1) * BANK], start=True, stop=True)
                ins.then_inc(bc_ready, 1)
                pe.wait_ge(xn_done, n(xn_done, TB))
                transposes(xn)
                pe.wait_ge(row_read, n(row_read))
                row_broadcast()
                pe.wait_ge(xt_done, n.last(xt_done))
                for tb in range(TB):
                    for c in range(DC):
                        ins = pe.matmul(ps[:, 4, 8 * tb:8 * tb + 8], xt[:, c * TOKENS + tb * P:c * TOKENS + tb * P + P], r_w[:, c, :],
                                        start=c == 0, stop=c == DC - 1)
                ins.then_inc(mo_lg, 1)
                pe.wait_ge(mo_sel, n(mo_sel))
                s0, s1 = r_q[:, R_SEL, :], r_q[:, R_SEL + 1, :]
                pe.matmul(ps[:, 4, 16:24], strict, s0, start=True, stop=True)
                pe.matmul(ps[:, 4, 24:32], ones, s0, start=True, stop=False)
                pe.matmul(ps[:, 4, 24:32], strict, s1, start=False, stop=True)
                pe.matmul(ps[:, 4, 32:40], ones, s0, start=True, stop=False)
                pe.matmul(ps[:, 4, 32:40], ones, s1, start=False, stop=True).then_inc(mo_rank, 1)
                def gather():
                    pe.wait_ge(mo_p, n(mo_p))
                    for k in range(2):
                        for c in range(4):
                            for tb in range(TB):
                                ins = pe.matmul(ps[:, 5 + 2 * k, c * P:(c + 1) * P], xn[:, tb, (4 * k + c) * P:(4 * k + c + 1) * P],
                                                mo_P[:, tb, :], start=tb == 0, stop=tb == TB - 1)
                        ins.then_inc(mo_x, 1)

                def spread():
                    for tb in range(TB):
                        for nh in range(2):
                            ins = pe.matmul(ps[:, (2 if tb == 0 else 5) + (1 + tb) * nh, :], mo_PT[:, tb, :], mo_ye[:, nh * BANK:(nh + 1) * BANK],
                                            start=True, stop=True)
                    return ins

                gather()
                pe.wait_ge(mo_ids, n(mo_ids))
                n_blocks = pe.value_load(eid[0:1, 11:12], min_val=N_EXPERTS, max_val=N_EXPERTS + MAX_EXTRA)
                with pe.Fori(0, n_blocks) as b:
                    start_blocks(n, b)

                    def beside(i):
                        if i == SPREAD_AT:
                            pe.wait_ge(mo_y, n(mo_y))
                            pe.wait_ge(mo_ptc, b + 1)
                            spread().then_inc(mo_c, 1)
                        if i == GATES_AT:
                            pe.wait_ge(mo_cc, n(mo_cc))
                            for tb in range(TB):
                                ins = pe.transpose(ps[:, 3, tb * P:(tb + 1) * P], mo_PG[:, tb, :], ident)
                            ins.then_inc(mo_pt, 1)
                        if i == GATHER_AT:
                            gather()
                    pe.wait_ge(mo_xl, n(mo_xl, 2))
                    gated(FF2, 1, beside)
                    end_blocks(n)
                pe.transpose(ps[:, 2, 0:P], ident, ident).then_inc(mo_end, 1)
                pe.wait_ge(mo_end_y, n(mo_end_y))
                spread().then_inc(mo_end_c, 1)

            pe.wait_ge(boot, BOOT)
            pe.transpose(ps[:, 0, 0:ROWS_A], scr[0:ROWS_A, 0:P], ident[0:ROWS_A, 0:ROWS_A])
            pe.transpose(ps[:, 1, 0:96], scr[0:96, P:2 * P], ident[0:96, 0:96])
            pe.transpose(ps[:, 3, 0:96], scr[0:96, 3 * P:4 * P], ident[0:96, 0:96])
            pe.transpose(ps[:, 2, 0:P], scr[:, 2 * P:3 * P], ident).then_inc(rows_t, 1)
            norm(lead=True)
            gated(FF1)
            row_broadcast()
            norm()
            even()
            norm(lead=True)
            gated(FF1)
            row_broadcast()
            norm(lead=True)
            gated(FF1)
            row_broadcast()
            mod_columns(0, 0)
            mod_columns(0, 1)
            norm()
            odd()
            norm(lead=True)
            gated(FF1)
            row_broadcast()
            norm()
            norm()
            diff_attention()
            norm(lead=True)
            gated(FF2)
            row_broadcast()
            mod_columns(1, 0)
            fourier()
            experts()




_INS = ["x", "norm_w", "ffn_w_gate", "ffn_w_up", "ffn_w_down", "even_w_in", "even_conv_w", "even_a_log",
        "even_dt_bias", "even_head_norm_w", "even_w_out", "odd_w_in", "odd_conv_w", "odd_conv_b", "odd_dt_bias",
        "odd_a_log", "odd_d_skip", "odd_out_norm_w", "odd_w_out", "c_2", "ctx_2", "c_ctx_2", "ada_w_2", "ada_b_2",
        "norm1_g_2", "norm2_g_2", "attn_w_qkv_2", "attn_lq1_2", "attn_lk1_2", "attn_lq2_2", "attn_lk2_2",
        "attn_subln_g_2", "attn_w_o_2", "fnet_w_o_2", "fnet_b_o_2", "ff_w1_2", "ff_w3_2", "ff_w2_2",
        "moe_router_2", "moe_w1_2", "moe_w3_2", "moe_w2_2", "final_g_2"]


def kernel(**inputs):
    import numpy as _np
    import concourse.bacc as _bacc
    from concourse.bass_utils import run_bass_kernel_spmd as _run

    nc = _bacc.Bacc("TRN2", target_bir_lowering=False, num_devices=1, dynamic_dma_scratch_size=1024)
    arrays, args = {}, {}
    for name in _INS:
        a = _np.ascontiguousarray(inputs[name])
        arrays[f"in_{name}"] = a
        args[name] = nc.dram_tensor(f"in_{name}", a.shape, mybir.dt.from_np(a.dtype), kind="ExternalInput").ap()
    c = host_constants()
    arrays["constants"] = c
    const = nc.dram_tensor("constants", c.shape, F32, kind="ExternalInput").ap()
    out = nc.dram_tensor("out", (1, TOKENS, DM), F32, kind="ExternalOutput").ap()
    build_block_kernel(nc, args, const, out)
    r = _run(nc, [arrays], core_ids=[0])
    return r.results[0]["out"]
```
